# Optimizing a Trainium2 kernel written in Bass

```python
import jax, jax.numpy as jnp
from jax import lax
import numpy as np

D_MODEL = 1024
BATCH = 1
SEQ = 256
DEPTH = 1

CONV_WIDTH = 512
CONV_KERNEL = 3
N_HEADS = 8
HEAD_DIM = 64
ATTN_WIDTH = N_HEADS * HEAD_DIM
MOBA_BLOCK = 256
MOBA_TOPK = 3
QUERY_CHUNK = 32
N_GROUPS = 4
EXPERTS_PER_GROUP = 8
N_EXPERTS = N_GROUPS * EXPERTS_PER_GROUP
EXPERT_TOPK = 2
D_EXPERT = 256
LN_EPS = 1e-5
IN_COLS = 3 * CONV_WIDTH + 3 * ATTN_WIDTH + 2 * D_MODEL
SPLITS = [CONV_WIDTH, 2 * CONV_WIDTH, 3 * CONV_WIDTH,
          3 * CONV_WIDTH + ATTN_WIDTH, 3 * CONV_WIDTH + 2 * ATTN_WIDTH,
          3 * CONV_WIDTH + 3 * ATTN_WIDTH, 3 * CONV_WIDTH + 3 * ATTN_WIDTH + D_MODEL]

kernel_name = 'hybrid_conv_moba_hmoe'

def layer_norm(x, g, b):
    xf = x.astype(jnp.float32)
    mu = jnp.mean(xf, axis=-1, keepdims=True)
    var = jnp.mean(jnp.square(xf - mu), axis=-1, keepdims=True)
    return ((xf - mu) * lax.rsqrt(var + LN_EPS) * g + b).astype(x.dtype)

def causal_depthwise_conv(u, w):
    return lax.conv_general_dilated(
        u, w[:, None, :].astype(u.dtype), window_strides=(1,),
        padding=[(CONV_KERNEL - 1, 0)], dimension_numbers=('NWC', 'WIO', 'NWC'),
        feature_group_count=u.shape[-1])

def alibi_slopes():
    return jnp.asarray(2.0 ** (-8.0 * np.arange(1, N_HEADS + 1) / N_HEADS), jnp.float32)

def moba_attention(q, k, v, slopes):
    nb_, h_, s_, hd = q.shape
    s_pad = -(-s_ // MOBA_BLOCK) * MOBA_BLOCK
    pad = ((0, 0), (0, 0), (0, s_pad - s_), (0, 0))
    nblk = s_pad // MOBA_BLOCK
    kb = jnp.pad(k, pad).reshape(nb_, h_, nblk, MOBA_BLOCK, hd)
    vb = jnp.pad(v, pad).reshape(nb_, h_, nblk, MOBA_BLOCK, hd)
    kmean = jnp.mean(kb, axis=3)
    topk = min(MOBA_TOPK, nblk)
    n_chunks = s_ // QUERY_CHUNK
    qc = q.reshape(nb_, h_, n_chunks, QUERY_CHUNK, hd).transpose(2, 0, 1, 3, 4)
    scale = HEAD_DIM ** -0.5
    bidx = jnp.arange(nb_)[:, None, None, None]
    hidx = jnp.arange(h_)[None, :, None, None]
    offs = jnp.arange(MOBA_BLOCK)
    blk_ids = jnp.arange(nblk)

    def chunk_step(args):
        ci, qi = args
        t = ci * QUERY_CHUNK + jnp.arange(QUERY_CHUNK)
        own = (ci * QUERY_CHUNK) // MOBA_BLOCK
        gate = jnp.einsum('bhqd,bhnd->bhqn', qi, kmean).astype(jnp.float32)
        gate = jnp.where(blk_ids < own, gate, -jnp.inf)
        _, sel = lax.top_k(gate, topk)
        sel_valid = sel < own
        k_sel = kb[bidx, hidx, sel]
        v_sel = vb[bidx, hidx, sel]
        pos_past = sel[..., None] * MOBA_BLOCK + offs
        s_past = jnp.einsum('bhqd,bhqnkd->bhqnk', qi, k_sel).astype(jnp.float32) * scale
        s_past = s_past - slopes[:, None, None, None] * (t[:, None, None] - pos_past)
        s_past = jnp.where(sel_valid[..., None], s_past, -jnp.inf)
        k_own = lax.dynamic_slice_in_dim(kb, own, 1, axis=2)[:, :, 0]
        v_own = lax.dynamic_slice_in_dim(vb, own, 1, axis=2)[:, :, 0]
        pos_own = own * MOBA_BLOCK + offs
        s_own = jnp.einsum('bhqd,bhkd->bhqk', qi, k_own).astype(jnp.float32) * scale
        s_own = s_own - slopes[:, None, None] * (t[:, None] - pos_own)
        s_own = jnp.where(pos_own <= t[:, None], s_own, -jnp.inf)
        scores = jnp.concatenate(
            [s_past.reshape(nb_, h_, QUERY_CHUNK, topk * MOBA_BLOCK), s_own], axis=-1)
        p = jax.nn.softmax(scores, axis=-1).astype(v.dtype)
        p_past = p[..., :topk * MOBA_BLOCK].reshape(nb_, h_, QUERY_CHUNK, topk, MOBA_BLOCK)
        p_own = p[..., topk * MOBA_BLOCK:]
        return (jnp.einsum('bhqnk,bhqnkd->bhqd', p_past, v_sel)
                + jnp.einsum('bhqk,bhkd->bhqd', p_own, v_own))

    out = lax.map(chunk_step, (jnp.arange(n_chunks), qc))
    return out.transpose(1, 2, 0, 3, 4).reshape(nb_, h_, s_, hd)

def hybrid_mixer(x, w_in, conv_w, w_out_conv, w_out_attn, w_o, slopes):
    nb_, s_, _ = x.shape
    proj = jnp.einsum('bsd,dc->bsc', x, w_in)
    c_b, c_c, c_x, q, k, v, g_a, g_b = jnp.split(proj, SPLITS, axis=-1)
    y_conv = jnp.einsum('bsc,cd->bsd', c_b * causal_depthwise_conv(c_c * c_x, conv_w), w_out_conv)
    heads = lambda z: z.reshape(nb_, s_, N_HEADS, HEAD_DIM).transpose(0, 2, 1, 3)
    o = moba_attention(heads(q), heads(k), heads(v), slopes)
    o = o.transpose(0, 2, 1, 3).reshape(nb_, s_, ATTN_WIDTH)
    y_attn = jnp.einsum('bsc,cd->bsd', o, w_out_attn)
    y = jax.nn.sigmoid(g_a) * y_conv + jax.nn.sigmoid(g_b) * y_attn
    return jnp.einsum('bsd,de->bse', y, w_o)

def hierarchical_moe(x, w_router_group, w_router_expert, w_gate, w_up, w_down):
    nb_, s_, d_ = x.shape
    xt = x.reshape(-1, d_)
    g_prob = jax.nn.softmax((xt @ w_router_group).astype(jnp.float32), axis=-1)
    g_top_p, g_top = lax.top_k(g_prob, 1)
    e_logits = (xt @ w_router_expert).astype(jnp.float32).reshape(-1, N_GROUPS, EXPERTS_PER_GROUP)
    e_in_group = jnp.take_along_axis(e_logits, g_top[:, :, None], axis=1)[:, 0]
    e_top_logit, e_top = lax.top_k(e_in_group, EXPERT_TOPK)
    gate = g_top_p * jax.nn.softmax(e_top_logit, axis=-1)
    expert_id = g_top * EXPERTS_PER_GROUP + e_top
    combine = jnp.sum(jax.nn.one_hot(expert_id, N_EXPERTS, dtype=jnp.float32)
                      * gate[..., None], axis=1)
    h = (jax.nn.silu(jnp.einsum('td,edf->tef', xt, w_gate))
         * jnp.einsum('td,edf->tef', xt, w_up)
         * combine[..., None].astype(x.dtype))
    return jnp.einsum('tef,efd->td', h, w_down).reshape(nb_, s_, d_)

def setup_inputs(seed: int = 0) -> dict:
    key = jax.random.key(seed)
    ks = jax.random.split(key, 16)
    beta = (8.0 * DEPTH) ** -0.25
    nrm = lambda k, shape, sc: jax.random.normal(k, shape, jnp.float32) * sc
    ones = lambda n: jnp.ones((n,), jnp.float32)
    col_scale = jnp.concatenate([
        ones(CONV_WIDTH), ones(CONV_WIDTH), beta * ones(CONV_WIDTH),
        ones(ATTN_WIDTH), ones(ATTN_WIDTH), beta * ones(ATTN_WIDTH), ones(2 * D_MODEL)])
    return {
        'x': nrm(ks[0], (BATCH, SEQ, D_MODEL), 1.0),
        'w_in': nrm(ks[1], (DEPTH, D_MODEL, IN_COLS), D_MODEL ** -0.5) * col_scale,
        'conv_w': nrm(ks[2], (DEPTH, CONV_KERNEL, CONV_WIDTH), CONV_KERNEL ** -0.5),
        'w_out_conv': nrm(ks[3], (DEPTH, CONV_WIDTH, D_MODEL), beta * CONV_WIDTH ** -0.5),
        'w_out_attn': nrm(ks[4], (DEPTH, ATTN_WIDTH, D_MODEL), beta * ATTN_WIDTH ** -0.5),
        'w_o': nrm(ks[5], (DEPTH, D_MODEL, D_MODEL), beta * D_MODEL ** -0.5),
        'ln1_g': 1.0 + nrm(ks[6], (DEPTH, D_MODEL), 0.02),
        'ln1_b': nrm(ks[7], (DEPTH, D_MODEL), 0.02),
        'w_router_group': nrm(ks[8], (DEPTH, D_MODEL, N_GROUPS), D_MODEL ** -0.5),
        'w_router_expert': nrm(ks[9], (DEPTH, D_MODEL, N_EXPERTS), D_MODEL ** -0.5),
        'w_gate': nrm(ks[10], (DEPTH, N_EXPERTS, D_MODEL, D_EXPERT), beta * D_MODEL ** -0.5),
        'w_up': nrm(ks[11], (DEPTH, N_EXPERTS, D_MODEL, D_EXPERT), beta * D_MODEL ** -0.5),
        'w_down': nrm(ks[12], (DEPTH, N_EXPERTS, D_EXPERT, D_MODEL), beta * D_EXPERT ** -0.5),
        'ln2_g': 1.0 + nrm(ks[13], (DEPTH, D_MODEL), 0.02),
        'ln2_b': nrm(ks[14], (DEPTH, D_MODEL), 0.02),
    }

def reference(x, w_in, conv_w, w_out_conv, w_out_attn, w_o, ln1_g, ln1_b,
              w_router_group, w_router_expert, w_gate, w_up, w_down, ln2_g, ln2_b):
    alpha = (2.0 * DEPTH) ** 0.25
    slopes = alibi_slopes()
    for l in range(DEPTH):
        mix = hybrid_mixer(x, w_in[l], conv_w[l], w_out_conv[l], w_out_attn[l], w_o[l], slopes)
        x = layer_norm(alpha * x + mix, ln1_g[l], ln1_b[l])
        ffn = hierarchical_moe(x, w_router_group[l], w_router_expert[l], w_gate[l], w_up[l], w_down[l])
        x = layer_norm(alpha * x + ffn, ln2_g[l], ln2_b[l])
    return x


_drawn_inputs = setup_inputs


def setup_inputs(seed=0):
    import zlib

    import numpy as np

    out = dict(_drawn_inputs(seed))
    spreads = {}
    factors = {'ln1_b': 2.755, 'ln2_g': 7.51, 'ln2_b': 7.873, 'ln1_g': 2.675}
    for name, (base, spread) in spreads.items():
        noise = np.random.default_rng([zlib.crc32(name.encode()), seed]).standard_normal(out[name].shape)
        drawn = base * np.exp(spread * noise) if base else spread * noise
        out[name] = __import__('jax').numpy.asarray(drawn.astype(out[name].dtype))
    for name, factor in factors.items():
        out[name] = (out[name] * factor).astype(out[name].dtype)
    return out
```

```python
import numpy as np
import concourse.bass as bass
from concourse import mybir
from contextlib import ExitStack

F32 = mybir.dt.float32
F32R = mybir.dt.float32r
I32 = mybir.dt.int32
ALU = mybir.AluOpType
ACT = mybir.ActivationFunctionType
AX = mybir.AxisListType

P = 128
SEQ, DM = 256, 1024
TT = SEQ // P
KC = DM // P
CW, AW = 512, 512
CC = CW // P
NH, HD = 8, 64
NG, EPG, DE = 4, 8, 256
NE = NG * EPG
FC = DE // P
QE = 4
NQ = NE // QE
SLOTS = P // QE
NL = NG + NE
EPS = 1e-5
ALPHA = 2.0 ** 0.25
SCALE = HD ** -0.5
MASKED = -1e30
MAX_ROUNDS = NQ + TT * SEQ // SLOTS
N_CONSTS = 10
FAR = 1e6
COL_B, COL_C, COL_X, COL_Q, COL_K, COL_V = (CW * i for i in range(6))
COL_GA = 3 * CW + 3 * AW
COL_GB = COL_GA + DM
GRP = 2 * P
NRAW, NSPL = 2, 4
HALF = 512


def hybrid_block(nc, x, w_in, conv_w, w_out_conv, w_out_attn, w_o, ln1_g, ln1_b,
                 w_router_group, w_router_expert, w_gate, w_up, w_down, ln2_g, ln2_b, out):
    x_v = x[0, :, :].rearrange("(t p) d -> p t d", p=P)
    out_v = out[0, :, :].rearrange("(t p) d -> p t d", p=P)
    win_v = w_in[0, :, :].rearrange("(p k) c -> p k c", k=KC)
    wc_v = w_out_conv[0, :, :].rearrange("(j p) d -> p j d", p=P)
    wa_v = w_out_attn[0, :, :].rearrange("(j p) d -> p j d", p=P)
    wo_v = w_o[0, :, :].rearrange("(j p) d -> p j d", p=P)
    convw_v = conv_w[0, :, :].rearrange("i (j p) -> p j i", p=P)
    wrg_v = w_router_group[0, :, :].rearrange("(p k) g -> p k g", k=KC)
    wre_v = w_router_expert[0, :, :].rearrange("(p k) e -> p k e", k=KC)
    wg_v = w_gate[0, :, :, :].rearrange("e (p k) f -> p e k f", k=KC)
    wu_v = w_up[0, :, :, :].rearrange("e (p k) f -> p e k f", k=KC)
    wd_v = w_down[0, :, :, :].rearrange("e (j p) d -> p e j d", p=P)

    ctx = ExitStack()
    with ctx:
        def sb(name, shape, dt=F32, where=ctx):
            return where.enter_context(nc.sbuf_tensor(name, shape, dt))

        def sem(name):
            return ctx.enter_context(nc.semaphore(name))

        x1 = sb("x1", [P, TT, DM])
        wr = sb("wr", [P, KC, NL])
        convw = sb("convw", [P, CC, 3])
        ident = sb("ident", [P, P])
        alpha_i = sb("alpha_i", [P, P])
        before = sb("before", [P, P])
        ones = sb("ones", [P, P])
        slot_id = sb("slot_id", [P, SLOTS])
        group_key = sb("group_key", [P, NG])
        expert_key = sb("expert_key", [P, NE])
        half_neg = sb("half_neg", [P, TT])
        stats = sb("stats", [P, TT, 2, 6])
        moments = sb("moments", [P, TT, 2])
        rstd = sb("rstd", [P, TT])
        shift = sb("shift", [P, TT])
        rt = sb("rt", [P, 16, TT, NE])
        rs = sb("rs", [P, 16, TT])
        rounds_f = sb("rounds_f", [P, 4, 16])
        rounds_i = sb("rounds_i", [P, 1, 16], I32)
        bounds = sb("bounds", [P, 16], I32)
        rank = sb("rank", [P, TT, NE])
        comb = sb("comb", [P, TT, NE])

        gu0 = sb("gu0", [P, QE, KC, 2 * DE])
        dn_scope = ExitStack()
        qT = sb("qT", [P, CC, SEQ], where=dn_scope)
        kT = sb("kT", [P, CC, SEQ], where=dn_scope)
        vv = sb("vv", [P, TT, AW], where=dn_scope)
        dist = sb("dist", [P, 3, P], where=dn_scope)
        sc = sb("sc", [P, 2, 3, P], where=dn_scope)
        pT = sb("pT", [P, 2, 3, P], where=dn_scope)
        nmax = sb("nmax", [P, 2, 2], where=dn_scope)
        rsum = sb("rsum", [P, 2, 2], where=dn_scope)
        rinv = sb("rinv", [P, 2, 2], where=dn_scope)
        cc_t = sb("cc_t", [P, 2, SEQ], where=dn_scope)
        u_t = sb("u_t", [P, 2, 2 + SEQ], where=dn_scope)
        cv_t = sb("cv_t", [P, 2, SEQ], where=dn_scope)
        z_t = sb("z_t", [P, SEQ], where=dn_scope)
        dn_scope.close()
        dn = sb("dn", [P, QE, FC, DM])

        mix_scope = ExitStack()
        xh = sb("xh", [P, KC, SEQ], F32R, mix_scope)
        xl = sb("xl", [P, KC, SEQ], F32R, mix_scope)
        raw = sb("raw", [P, NRAW, KC * GRP], where=mix_scope)
        wh = sb("wh", [P, NSPL, KC * P], F32R, mix_scope)
        wl = sb("wl", [P, NSPL, KC * P], F32R, mix_scope)
        zh = sb("zh", [P, CC, SEQ], F32R, mix_scope)
        zl = sb("zl", [P, CC, SEQ], F32R, mix_scope)
        oh = sb("oh", [P, CC, SEQ], F32R, mix_scope)
        ol = sb("ol", [P, CC, SEQ], F32R, mix_scope)
        yh = sb("yh", [P, 2, SEQ], F32R, mix_scope)
        yl = sb("yl", [P, 2, SEQ], F32R, mix_scope)
        sig = sb("sig", [P, 2, 2 * SEQ], where=mix_scope)
        yt = sb("yt", [P, 2, SEQ], where=mix_scope)
        mix_scope.close()
        lng = sb("lng", [P, DM])
        lnb = sb("lnb", [P, DM])
        gu1 = sb("gu1", [P, QE, KC, 2 * DE])
        x1T = sb("x1T", [P, KC, SEQ])
        xg = sb("xg", [P, KC, P])
        pick = sb("pick", [P, TT, QE, SLOTS])
        pickw = sb("pickw", [P, TT, QE, SLOTS])
        put = sb("put", [P, SEQ])
        sg = sb("sg", [P, DE])
        hs = sb("hs", [P, DE])
        hT = sb("hT", [P, FC, P])
        ys = sb("ys", [P, DM])

        bank = [ctx.enter_context(nc.psum_tensor(f"bank{i}", [P, HALF], F32)) for i in range(8)]

        gu = [gu0, gu1]

        x_in = sem("x_in")
        small_in = sem("small_in")
        raw_in = [sem(f"raw_in{i}") for i in range(NRAW)]
        ln_in = sem("ln_in")
        gu_in = [sem(f"gu_in{i}") for i in range(2)]
        dn_in = sem("dn_in")
        out_done = sem("out_done")
        zeroed = sem("zeroed")
        consts = sem("consts")
        pool_link = sem("pool_link")
        xT_ps = sem("xT_ps")
        xh_done = sem("xh_done")
        xl_done = sem("xl_done")
        hi_done = sem("hi_done")
        lo_done = sem("lo_done")
        unit_done = sem("unit_done")
        evac_a = sem("evac_a")
        evac_v = sem("evac_v")
        score_ps = sem("score_ps")
        score_sb = sem("score_sb")
        exp_done = sem("exp_done")
        prob_done = sem("prob_done")
        pT_ps = sem("pT_ps")
        pT_done = sem("pT_done")
        pv_ps = sem("pv_ps")
        oh_done = sem("oh_done")
        ol_done = sem("ol_done")
        z_done = sem("z_done")
        zh_done = sem("zh_done")
        zl_done = sem("zl_done")
        sig_done = sem("sig_done")
        y_done = sem("y_done")
        yh_done = sem("yh_done")
        yl_done = sem("yl_done")
        dve_link = sem("dve_link")
        nmax_done = sem("nmax_done")
        moment_done = sem("moment_done")
        rstd_done = sem("rstd_done")
        shift_done = sem("shift_done")
        norm_done = sem("norm_done")
        x1_done = sem("x1_done")
        x1T_ps = sem("x1T_ps")
        logit_ps = sem("logit_ps")
        gexp_in = sem("gexp_in")
        gexp_done = sem("gexp_done")
        routed = sem("routed")
        rank_ps = sem("rank_ps")
        rounds_done = sem("rounds_done")
        rank_read = sem("rank_read")
        y_link = sem("y_link")
        round_link = sem("round_link")
        bank_free = {b: sem(f"bank_free{b}") for b in (4, 5, 6, 7)}
        pick_done = sem("pick_done")
        xg_ps = sem("xg_ps")
        xg_a = sem("xg_a")
        xg_v = sem("xg_v")
        put_ps = sem("put_ps")
        put_done = sem("put_done")
        gu_ps = sem("gu_ps")
        sg_done = sem("sg_done")
        h_done = sem("h_done")
        hT_ps = sem("hT_ps")
        hT_done = sem("hT_done")
        y_ps = sem("y_ps")
        ys_a = sem("ys_a")
        ys_v = sem("ys_v")
        added = sem("added")
        gu_free = [sem(f"gu_free{i}") for i in range(2)]
        dn_free = sem("dn_free")
        out_sb = sem("out_sb")

        phase_a = ([("q", 0), ("q", 1), ("k", 0), ("k", 1), ("v", 0), ("v", 1)]
                   + [(n, c) for c in range(CC // 2) for n in ("cc", "cx", "cb")])
        lead = [("ga", 0), ("gb", 0)]
        NA = len(phase_a)
        PB = NA + len(lead)
        JP = KC // 2
        START = {"q": COL_Q, "k": COL_K, "v": COL_V, "cc": COL_C, "cx": COL_X, "cb": COL_B,
                 "ga": COL_GA, "gb": COL_GB}

        sequence = (phase_a + lead
                    + [x for j in range(JP - 1) for x in (("ca", j), ("ga", j + 1), ("gb", j + 1), ("wo", j))]
                    + [("ca", JP - 1), ("wo", JP - 1)])
        UNITS = 2 * len(sequence)
        U0 = 2 * PB
        UPJ = 8
        UA = 12
        assert U0 % NSPL == 0 and PB % NRAW == 0 and UPJ % NSPL == 0

        def unit(n):
            return sequence[n // 2][0], 2 * sequence[n // 2][1] + n % 2

        def evacuated(n):
            mine = ("q", "k", "v", "cc")
            on_act = unit(n)[0] in mine
            return on_act, sum((unit(m)[0] in mine) == on_act for m in range(n + 1))

        block = ctx.enter_context(nc.Block())

        @block.sync
        def _(sp):
            def load_pair(slot, kind, idx):
                s = raw_in[slot]
                dst = raw[:, slot, :].rearrange("p (k c) -> p k c", k=KC)
                if kind in START:
                    for k in (0, KC // 2):
                        sp.dma_start(dst[:, k:k + KC // 2, :],
                                     win_v[:, k:k + KC // 2, bass.ds(idx * GRP + START[kind], GRP)]
                                     ).then_inc(s, 16)
                elif kind == "ca":
                    sp.dma_start(dst[:, 0:CC, :], wc_v[:, :, bass.ds(idx * GRP, GRP)]).then_inc(s, 16)
                    sp.dma_start(dst[:, CC:KC, :], wa_v[:, :, bass.ds(idx * GRP, GRP)]).then_inc(s, 16)
                else:
                    for i in range(2):
                        sp.dma_start(dst[:, :, i * P:(i + 1) * P],
                                     wo_v[:, bass.ds(idx * 2 + i, 1), :].rearrange(
                                         "p a (k c) -> p (a k) c", k=KC)).then_inc(s, 16)

            def load_gu(h, q):
                for e in range(QE):
                    sp.dma_start(gu[h][:, e, :, 0:DE],
                                 wg_v[:, bass.ds(q * QE + e, 1), :, :]).then_inc(gu_in[h], 16)
                    sp.dma_start(gu[h][:, e, :, DE:2 * DE],
                                 wu_v[:, bass.ds(q * QE + e, 1), :, :]).then_inc(gu_in[h], 16)

            def load_dn(q):
                for e in range(QE):
                    sp.dma_start(dn[:, e, :, :],
                                 wd_v[:, bass.ds(q * QE + e, 1), :, :]).then_inc(dn_in, 16)

            for t in range(TT):
                sp.dma_start(x1[:, t, :], x_v[:, t, :]).then_inc(x_in, 16)
            for n in range(PB):
                if n >= NRAW:
                    sp.wait_ge(lo_done, 2 * (n - NRAW + 1))
                load_pair(n % NRAW, *sequence[n])
            with sp.Fori(0, JP - 1) as j:
                for i, (kind, idx) in enumerate((("ca", j), ("ga", j + 1), ("gb", j + 1), ("wo", j))):
                    sp.wait_ge(lo_done, UPJ * j + 2 * (PB + i - NRAW + 1))
                    load_pair((PB + i) % NRAW, kind, idx)
            for n in range(len(sequence) - 2, len(sequence)):
                sp.wait_ge(lo_done, 2 * (n - NRAW + 1))
                load_pair(n % NRAW, *sequence[n])
            load_gu(0, 0)
            sp.wait_ge(pv_ps, CC)
            sp.wait_ge(zl_done, CC)
            load_dn(0)
            sp.wait_ge(unit_done, UNITS)
            load_gu(1, 1)
            sp.wait_ge(dn_free, 1)
            load_dn(1)
            with sp.Fori(1, NQ // 2) as o:
                for h in range(2):
                    sp.wait_ge(gu_free[h], o)
                    load_gu(h, 2 * o + h)
                    sp.wait_ge(dn_free, 2 * o + h)
                    load_dn(2 * o + h)
            for t in range(TT):
                sp.wait_ge(x1_done, TT + t + 1)
                sp.dma_start(out_v[:, t, :], x1[:, t, :]).then_inc(out_done, 16)
            sp.wait_ge(out_done, 16 * TT)

        @block.gpsimd
        def _(pool):
            linked = [0]

            def link(ins):
                linked[0] += 1
                ins.then_inc(pool_link, 1)
                pool.wait_ge(pool_link, linked[0])

            def const(ins):
                ins.then_inc(consts, 1)

            link(pool.memset(ident[:, :], 0.0))
            const(pool.affine_select(out=ident[:, :], in_=ident[:, :], compare_op=ALU.not_equal,
                                     fill=1.0, base=0, pattern=[[-1, P]], channel_multiplier=1))
            link(pool.iota(dist[:, 0, :], pattern=[[1, P]], base=0, channel_multiplier=-1,
                           allow_small_or_imprecise_dtypes=True))
            link(pool.affine_select(out=dist[:, 0, :], in_=dist[:, 0, :], compare_op=ALU.is_ge,
                                    fill=MASKED, base=0, pattern=[[-1, P]], channel_multiplier=1))
            const(pool.iota(dist[:, 1, :], pattern=[[1, P]], base=-P, channel_multiplier=-1,
                            allow_small_or_imprecise_dtypes=True))
            const(pool.tensor_copy(dist[:, 2, :], dist[:, 0, :]))
            link(pool.memset(alpha_i[:, :], 0.0))
            const(pool.affine_select(out=alpha_i[:, :], in_=alpha_i[:, :], compare_op=ALU.not_equal,
                                     fill=ALPHA, base=0, pattern=[[-1, P]], channel_multiplier=1))
            link(pool.memset(before[:, :], 1.0))
            const(pool.affine_select(out=before[:, :], in_=before[:, :], compare_op=ALU.is_gt, fill=0.0,
                                     base=0, pattern=[[1, P]], channel_multiplier=-1))
            const(pool.memset(ones[:, :], 1.0))
            const(pool.iota(slot_id[:, :], pattern=[[1, SLOTS]], base=0, channel_multiplier=0,
                            allow_small_or_imprecise_dtypes=True))
            const(pool.iota(group_key[:, :], pattern=[[-1, NG]], base=NG, channel_multiplier=0,
                            allow_small_or_imprecise_dtypes=True))
            const(pool.iota(expert_key[:, :], pattern=[[-1, NE]], base=NE, channel_multiplier=0,
                            allow_small_or_imprecise_dtypes=True))
            const(pool.memset(half_neg[:, :], -0.5))
            pool.wait_ge(consts, N_CONSTS)
            for n, (g, b) in enumerate(((ln1_g, ln1_b), (ln2_g, ln2_b))):
                if n == 0:
                    pool.wait_ge(unit_done, UNITS - 6)
                else:
                    pool.wait_ge(x1_done, TT)
                pool.dma_start(lng[:, :], g[0:1, :].broadcast_to([P, DM])).then_inc(ln_in, 16)
                pool.dma_start(lnb[:, :], b[0:1, :].broadcast_to([P, DM])).then_inc(ln_in, 16)
                pool.wait_ge(moment_done, n + 1)
                pool.tensor_tensor(rstd[:, :], moments[:, :, 1], half_neg[:, :],
                                   ALU.pow).then_inc(rstd_done, 1)

        @block.scalar
        def _(act):
            for i in range(3):
                act.dma_start(convw[:, :, i], convw_v[:, :, i],
                              allow_slow_non_contiguous=True).then_inc(small_in, 16)
            act.dma_start(wr[:, :, 0:NG], wrg_v, allow_slow_non_contiguous=True).then_inc(small_in, 16)
            act.dma_start(wr[:, :, NG:NL], wre_v, allow_slow_non_contiguous=True).then_inc(small_in, 16)

            def high(n, j=None):
                pair, s, more = n // 2, n % NSPL, 0 if j is None else j
                if n % 2 == 0:
                    act.wait_ge(raw_in[pair % NRAW], more * 16 * UPJ // NRAW + 32 * (pair // NRAW + 1))
                if n >= NSPL:
                    act.wait_ge(unit_done, more * UPJ + n - NSPL + 1)
                act.activation(wh[:, s, :].rearrange("p (k c) -> p k c", k=KC),
                               raw[:, pair % NRAW, :].rearrange("p (k c) -> p k c", k=KC)
                               [:, :, n % 2 * P:(n % 2 + 1) * P], ACT.Copy).then_inc(hi_done, 1)

            def attention(i):
                c, stage = i // 3, i % 3
                if stage == 0 and 1 <= c <= CC:
                    act.wait_ge(pv_ps, c)
                    act.activation(oh[:, c - 1, :], bank[6 + (c - 1) % 2][:, 0:SEQ],
                                   ACT.Copy).then_inc(oh_done, 1)
                if c >= CC:
                    return
                for j in range(2):
                    if stage == 0:
                        act.wait_ge(nmax_done, 2 * c + j + 1)
                        act.activation(sc[:, j, 0, :], sc[:, j, 0, :], ACT.Exp, bias=nmax[:, j, 0:1],
                                       accum_out=rsum[:, j, 0:1])
                        act.activation(sc[:, j, 1:3, :], sc[:, j, 1:3, :], ACT.Exp,
                                       bias=nmax[:, j, 1:2], accum_out=rsum[:, j, 1:2]
                                       ).then_inc(exp_done, 1)
                    if stage == 2:
                        act.wait_ge(pT_ps, 2 * c + j + 1)
                        if c >= 1:
                            act.wait_ge(pv_ps, c)
                        act.activation(pT[:, j, :, :],
                                       bank[2 + j][:, 0:3 * P].rearrange("p (b q) -> p b q", b=3),
                                       ACT.Copy).then_inc(pT_done, 1)

            for n in range(NSPL):
                high(n)
            for b in range(KC // 2):
                act.wait_ge(xT_ps, b + 1)
                act.activation(xh[:, 2 * b:2 * b + 2, :],
                               bank[b][:, :].rearrange("p (k s) -> p k s", k=2),
                               ACT.Copy).then_inc(xh_done, 1)

            for n in range(U0):
                kind, c = unit(n)
                src = bank[4 + n % 2][:, 0:SEQ]
                if kind in ("q", "k", "v", "cc"):
                    act.wait_ge(unit_done, n + 1)
                if kind == "q":
                    act.activation(qT[:, c, :], src, ACT.Copy, scale=SCALE).then_inc(evac_a, 1)
                elif kind == "k":
                    act.activation(kT[:, c, :], src, ACT.Copy).then_inc(evac_a, 1)
                elif kind == "v":
                    act.activation(vv[:, :, c * P:(c + 1) * P],
                                   src.rearrange("p (t c) -> p t c", t=TT), ACT.Copy).then_inc(evac_a, 1)
                elif kind == "cc":
                    if c >= 2:
                        act.wait_ge(evac_v, evacuated(n - 4)[1])
                    act.activation(cc_t[:, c % 2, :], src, ACT.Copy).then_inc(evac_a, 1)
                high(n + NSPL)
                if kind == "cb":
                    act.wait_ge(z_done, c + 1)
                    act.activation(zh[:, c, :], z_t[:, :], ACT.Copy).then_inc(zh_done, 1)
                if n >= UA:
                    attention(n - UA)

            def gates():
                for m in range(2):
                    act.activation(sig[:, m, :], bank[4 + m][:, :], ACT.Sigmoid).then_inc(sig_done, 1)

            def y_high(j, m):
                act.wait_ge(y_done, 2 * j + m + 1)
                act.activation(yh[:, m, :], yt[:, m, :], ACT.Copy).then_inc(yh_done, 1)

            act.wait_ge(unit_done, U0)
            gates()
            with act.Fori(0, JP - 1) as j:
                for i in range(UPJ):
                    high(U0 + i + NSPL, j)
                    if i in (1, 2):
                        y_high(j, i - 1)
                    if i == 5:
                        act.wait_ge(unit_done, UPJ * j + U0 + 6)
                        gates()
            for m in range(2):
                y_high(JP - 1, m)

            def norm(n):
                act.wait_ge(shift_done, n + 1)
                for t in range(TT):
                    for h in range(2):
                        act.activation(x1[:, t, h * HALF:(h + 1) * HALF], bank[2 * t + h][:, :],
                                       ACT.Identity, scale=rstd[:, t:t + 1],
                                       bias=shift[:, t:t + 1]).then_inc(norm_done, 1)

            norm(0)
            for m, b in enumerate((4, 7)):
                act.wait_ge(x1T_ps, b - 3)
                act.activation(x1T[:, 2 * (b - 4):2 * (b - 4) + 2, :],
                               bank[b][:, :].rearrange("p (k s) -> p k s", k=2),
                               ACT.Copy).then_inc(bank_free[b], 1)
            act.wait_ge(gexp_in, 1)
            act.activation(rt[:, 12, :, 0:NG + 1], rt[:, 11, :, 0:NG + 1], ACT.Exp).then_inc(gexp_done, 1)

            act.wait_ge(rounds_done, 1)
            with act.Fori(0, NQ) as q:
                first = act.value_load(bounds[0:1, bass.ds(q, 1)], min_val=0, max_val=MAX_ROUNDS)
                end = act.value_load(bounds[0:1, bass.ds(q + 1, 1)], min_val=1, max_val=MAX_ROUNDS)
                with act.Fori(first, end) as c:
                    act.wait_ge(xg_ps, 2 * c + 1)
                    act.activation(xg[:, 0:KC // 2, :], bank[4][:, :].rearrange("p (k s) -> p k s", s=P),
                                   ACT.Copy).then_inc(xg_a, 1)
                    act.wait_ge(put_ps, c + 1)
                    act.activation(put[:, :], bank[7][:, SEQ:2 * SEQ], ACT.Copy).then_inc(put_done, 1)
                    act.wait_ge(gu_ps, c + 1)
                    act.activation(sg[:, :], bank[6][:, 0:DE], ACT.Sigmoid).then_inc(sg_done, 1)
                    act.wait_ge(hT_ps, c + 1)
                    act.activation(hT[:, :, :], bank[7][:, 0:SEQ].rearrange("p (j s) -> p j s", j=FC),
                                   ACT.Copy).then_inc(bank_free[7], 1)
                    act.wait_ge(y_ps, 2 * c + 1)
                    act.activation(ys[:, 0:HALF], bank[4][:, :], ACT.Copy).then_inc(bank_free[4], 1)
            norm(1)

        @block.vector
        def _(dve):
            linked = [0]

            def link(ins):
                linked[0] += 1
                ins.then_inc(dve_link, 1)
                dve.wait_ge(dve_link, linked[0])

            def low(n, j=None):
                pair, s, more = n // 2, n % NSPL, 0 if j is None else j
                dve.wait_ge(hi_done, more * UPJ + n + 1)
                dve.tensor_tensor(wl[:, s, :].rearrange("p (k c) -> p k c", k=KC),
                                  raw[:, pair % NRAW, :].rearrange("p (k c) -> p k c", k=KC)
                                  [:, :, n % 2 * P:(n % 2 + 1) * P],
                                  wh[:, s, :].bitcast(F32).rearrange("p (k c) -> p k c", k=KC),
                                  ALU.subtract).then_inc(lo_done, 1)

            def attention(i):
                c, stage = i // 3, i % 3
                if stage == 0 and 1 <= c <= CC:
                    dve.wait_ge(oh_done, c)
                    dve.tensor_tensor(ol[:, c - 1, :], bank[6 + (c - 1) % 2][:, 0:SEQ],
                                      oh[:, c - 1, :].bitcast(F32), ALU.subtract).then_inc(ol_done, 1)
                if c >= CC:
                    return
                if stage == 0:
                    for j in range(2):
                        dve.wait_ge(score_ps, 2 * c + j + 1)
                        if c >= 1:
                            dve.wait_ge(pT_ps, 2 * c)
                        dve.scalar_tensor_tensor(
                            sc[:, j, :, :], dist[:, :, :], float(2.0 ** (-8.0 * (2 * c + j + 1) / NH)),
                            bank[j][:, 0:3 * P].rearrange("p (b k) -> p b k", b=3),
                            ALU.mult, ALU.add).then_inc(score_sb, 1)
                    for j in range(2):
                        dve.wait_ge(score_sb, 2 * c + j + 1)
                        dve.tensor_reduce(nmax[:, j, 0:1], sc[:, j, 0, :], AX.X, ALU.max, negate=True)
                        dve.tensor_reduce(nmax[:, j, 1:2], sc[:, j, 1:3, :], AX.XY, ALU.max,
                                          negate=True).then_inc(nmax_done, 1)
                if stage == 1:
                    dve.wait_ge(exp_done, 2 * c + 2)
                    link(dve.reciprocal(rinv[:, :, :], rsum[:, :, :]))
                    for j in range(2):
                        dve.tensor_scalar(sc[:, j, 0, :], sc[:, j, 0, :], rinv[:, j, 0:1], None, ALU.mult)
                        dve.tensor_scalar(sc[:, j, 1:3, :], sc[:, j, 1:3, :], rinv[:, j, 1:2], None,
                                          ALU.mult).then_inc(prob_done, 1)

            link(dve.memset(u_t[:, :, 0:2], 0.0))
            for n in range(NSPL):
                low(n)
            for b in range(KC // 2):
                dve.wait_ge(xh_done, b + 1)
                dve.tensor_tensor(xl[:, 2 * b:2 * b + 2, :],
                                  bank[b][:, :].rearrange("p (k s) -> p k s", k=2),
                                  xh[:, 2 * b:2 * b + 2, :].bitcast(F32),
                                  ALU.subtract).then_inc(xl_done, 1)
            dve.wait_ge(consts, N_CONSTS)
            dve.wait_ge(small_in, 80)
            for n in range(U0):
                kind, c = unit(n)
                src = bank[4 + n % 2][:, 0:SEQ]
                u, cv = u_t[:, c % 2, :], cv_t[:, c % 2, :]
                if kind == "cx":
                    dve.wait_ge(unit_done, n + 1)
                    dve.wait_ge(evac_a, evacuated(n - 2)[1])
                    dve.tensor_tensor(u[:, 2:], src, cc_t[:, c % 2, :], ALU.mult).then_inc(evac_v, 1)
                if kind == "cb":
                    dve.wait_ge(unit_done, n + 1)
                    dve.tensor_tensor(z_t[:, :], src, cv, ALU.mult).then_inc(evac_v, 1)
                    dve.wait_ge(evac_v, evacuated(n)[1])
                    dve.engine_nop().then_inc(z_done, 1)
                low(n + NSPL)
                if kind == "cx":
                    dve.wait_ge(evac_v, evacuated(n)[1])
                    link(dve.tensor_scalar(cv, u[:, 2:], convw[:, c, 2:3], None, ALU.mult))
                    link(dve.scalar_tensor_tensor(cv, u[:, 1:1 + SEQ], convw[:, c, 1:2], cv,
                                                  ALU.mult, ALU.add))
                    link(dve.scalar_tensor_tensor(cv, u[:, 0:SEQ], convw[:, c, 0:1], cv,
                                                  ALU.mult, ALU.add))
                if kind == "cb":
                    dve.wait_ge(zh_done, c + 1)
                    dve.tensor_tensor(zl[:, c, :], z_t[:, :], zh[:, c, :].bitcast(F32),
                                      ALU.subtract).then_inc(zl_done, 1)
                    dve.wait_ge(zl_done, c + 1)
                if n >= UA:
                    attention(n - UA)

            def y_chunk(j, m):
                dve.wait_ge(unit_done, UPJ * j + U0 + m + 1)
                dve.wait_ge(sig_done, 2 * j + m + 1)
                dve.tensor_tensor(sig[:, m, :], sig[:, m, :], bank[6 + m][:, :],
                                  ALU.mult).then_inc(y_link, 1)
                dve.wait_ge(y_link, 2 * j + m + 1)
                dve.tensor_tensor(yt[:, m, :], sig[:, m, 0:SEQ], sig[:, m, SEQ:2 * SEQ],
                                  ALU.add).then_inc(y_done, 1)

            def y_low(j, m):
                dve.wait_ge(yh_done, 2 * j + m + 1)
                dve.tensor_tensor(yl[:, m, :], yt[:, m, :], yh[:, m, :].bitcast(F32),
                                  ALU.subtract).then_inc(yl_done, 1)

            with dve.Fori(0, JP - 1) as j:
                for i in range(UPJ):
                    if i < 2:
                        y_chunk(j, i)
                    low(U0 + i + NSPL, j)
                    if i in (2, 3):
                        y_low(j, i - 2)
            for m in range(2):
                y_chunk(JP - 1, m)
            for m in range(2):
                y_low(JP - 1, m)

            def norm(n):
                for t in range(TT):
                    for h in range(2):
                        ins = dve.bn_stats(stats[:, t, h, :], bank[2 * t + h][:, :])
                link(ins)
                for t in range(TT):
                    ins = dve.bn_aggr(moments[:, t, :], stats[:, t, :, :])
                link(ins)
                dve.tensor_scalar(moments[:, :, 1], moments[:, :, 1], EPS, None,
                                  ALU.add).then_inc(moment_done, 1)
                dve.wait_ge(rstd_done, n + 1)
                dve.scalar_tensor_tensor(shift[:, :], moments[:, :, 0], -1.0, rstd[:, :],
                                         ALU.mult, ALU.mult).then_inc(shift_done, 1)
                dve.wait_ge(ln_in, 32 * (n + 1))
                for t in range(TT):
                    dve.wait_ge(norm_done, 2 * TT * n + 2 * (t + 1))
                    link(dve.tensor_tensor(x1[:, t, :], x1[:, t, :], lng[:, :], ALU.mult))
                    dve.tensor_tensor(x1[:, t, :], x1[:, t, :], lnb[:, :], ALU.add).then_inc(x1_done, 1)

            dve.wait_ge(unit_done, UNITS)
            norm(0)
            for b in (5, 6):
                dve.wait_ge(x1T_ps, b - 3)
                dve.tensor_copy(x1T[:, 2 * (b - 4):2 * (b - 4) + 2, :],
                                bank[b][:, :].rearrange("p (k s) -> p k s", k=2)
                                ).then_inc(bank_free[b], 1)

            def over(v, n):
                return v.unsqueeze(2).to_broadcast([P, TT, n])

            def row(v, n):
                return v.unsqueeze(1).to_broadcast([P, TT, n])

            def first_max(v, key, n, top, eq, hot, scratch):
                link(dve.tensor_reduce(top, v, AX.X, ALU.max))
                link(dve.tensor_tensor(eq, v, over(top, n), ALU.is_ge))
                link(dve.tensor_tensor(eq, eq, row(key, n), ALU.mult))
                link(dve.tensor_reduce(scratch, eq, AX.X, ALU.max))
                link(dve.tensor_tensor(hot, eq, over(scratch, n), ALU.is_equal))

            gl, el = rt[:, 0, :, 0:NG], rt[:, 1, :, :]
            eq, masked, hot1, hot2 = rt[:, 2, :, :], rt[:, 3, :, :], rt[:, 4, :, :], rt[:, 5, :, :]
            geq, ghot, pen = rt[:, 6, :, 0:NG], rt[:, 7, :, 0:NG], rt[:, 8, :, 0:NG]
            chosen, part = rt[:, 9, :, :], rt[:, 10, :, :]
            e_in, e_out = rt[:, 11, :, :], rt[:, 12, :, :]
            gtop, top1, top2, tmp = (rs[:, i, :] for i in range(4))
            gsum, w1, w2 = (rs[:, i, :] for i in range(4, 7))
            link(dve.memset(rounds_f[:, :, :], 0.0))
            dve.wait_ge(logit_ps, 1)
            logits = bank[0][:, 0:TT * NL].rearrange("p (t n) -> p t n", t=TT)
            dve.tensor_copy(el, logits[:, :, NG:NL])
            link(dve.tensor_copy(gl, logits[:, :, 0:NG]))
            first_max(gl, group_key[:, :], NG, gtop, geq, ghot, tmp)
            link(dve.tensor_scalar(pen, ghot, -MASKED, MASKED, ALU.mult, ALU.add))
            by_group = [v.rearrange("p t (g e) -> p t g e", g=NG) for v in (el, masked)]
            for t in range(TT):
                ghot_b, pen_b = (v[:, t, :].unsqueeze(2).to_broadcast([P, NG, EPG]) for v in (ghot, pen))
                link(dve.tensor_tensor(by_group[1][:, t, :, :], by_group[0][:, t, :, :], ghot_b, ALU.mult))
                link(dve.tensor_tensor(by_group[1][:, t, :, :], by_group[1][:, t, :, :], pen_b, ALU.add))
            first_max(masked, expert_key[:, :], NE, top1, eq, hot1, tmp)
            link(dve.scalar_tensor_tensor(masked, hot1, 100.0 * MASKED, masked, ALU.mult, ALU.add))
            first_max(masked, expert_key[:, :], NE, top2, eq, hot2, tmp)
            dve.tensor_tensor(chosen, hot1, hot2, ALU.add).then_inc(routed, 1)
            link(dve.tensor_tensor(e_in[:, :, 0:NG], gl, over(gtop, NG), ALU.subtract))
            dve.tensor_tensor(e_in[:, :, NG], top2, top1, ALU.subtract).then_inc(gexp_in, 1)
            dve.wait_ge(rank_ps, 1)
            ranks = bank[1][:, 0:TT * NE].rearrange("p (t n) -> p t n", t=TT)
            link(dve.scalar_tensor_tensor(rank[:, :, :], ranks, FAR, chosen, ALU.add, ALU.mult))
            link(dve.tensor_scalar(rank[:, :, :], rank[:, :, :], -FAR, None, ALU.add))
            counts = bank[1][0:1, TT * NE:(TT + 1) * NE].rearrange("p (q e) -> p q e", q=NQ)
            rf, ri = rounds_f[0:1, :, :], rounds_i[0:1, 0, 0:NQ]
            link(dve.tensor_reduce(rf[:, 0, NQ:2 * NQ], counts, AX.X, ALU.max))
            link(dve.tensor_scalar(ri, rf[:, 0, NQ:2 * NQ], float(SLOTS - 1), None, ALU.add))
            link(dve.tensor_scalar(ri, ri, SLOTS.bit_length() - 1, None, ALU.logical_shift_right))
            link(dve.tensor_scalar(rf[:, 0, NQ:2 * NQ], ri, 1.0, None, ALU.max))
            for i in range(3):
                d = 1 << i
                link(dve.tensor_tensor(rf[:, i + 1, NQ:2 * NQ], rf[:, i, NQ:2 * NQ],
                                       rf[:, i, NQ - d:2 * NQ - d], ALU.add))
            dve.tensor_copy(bounds[0:1, 0:NQ + 1], rf[:, 3, NQ - 1:2 * NQ]).then_inc(rounds_done, 1)
            dve.wait_ge(gexp_done, 1)
            link(dve.tensor_reduce(gsum, e_out[:, :, 0:NG], AX.X, ALU.add))
            link(dve.tensor_scalar(w1, e_out[:, :, NG], 1.0, None, ALU.add))
            link(dve.tensor_tensor(w1, w1, gsum, ALU.mult))
            link(dve.reciprocal(w1, w1))
            link(dve.tensor_tensor(w2, w1, e_out[:, :, NG], ALU.mult))
            link(dve.tensor_tensor(comb[:, :, :], hot1, over(w1, NE), ALU.mult))
            link(dve.tensor_tensor(part, hot2, over(w2, NE), ALU.mult))
            link(dve.tensor_tensor(comb[:, :, :], comb[:, :, :], part, ALU.add))

            dve.wait_ge(rounds_done, 1)
            with dve.Fori(0, NQ) as q:
                first = dve.value_load(bounds[0:1, bass.ds(q, 1)], min_val=0, max_val=MAX_ROUNDS)
                end = dve.value_load(bounds[0:1, bass.ds(q + 1, 1)], min_val=1, max_val=MAX_ROUNDS)
                with dve.Fori(first, end) as c:
                    for t in range(TT):
                        mine = rank[:, t, bass.ds(q * QE, QE)]
                        dve.tensor_tensor(pick[:, t, :, :],
                                          slot_id[:, :].unsqueeze(1).to_broadcast([P, QE, SLOTS]),
                                          mine.unsqueeze(2).to_broadcast([P, QE, SLOTS]),
                                          ALU.is_equal).then_inc(round_link, 1)
                    dve.wait_ge(round_link, 4 * c + 2)
                    for t in range(TT):
                        dve.tensor_tensor(pickw[:, t, :, :], pick[:, t, :, :],
                                          comb[:, t, bass.ds(q * QE, QE)].unsqueeze(2).to_broadcast(
                                              [P, QE, SLOTS]), ALU.mult).then_inc(pick_done, 1)
                    dve.tensor_scalar(rank[:, :, bass.ds(q * QE, QE)], rank[:, :, bass.ds(q * QE, QE)],
                                      float(-SLOTS), None, ALU.add).then_inc(round_link, 1)
                    dve.wait_ge(xg_ps, 2 * c + 2)
                    dve.tensor_copy(xg[:, KC // 2:KC, :],
                                    bank[5][:, :].rearrange("p (k s) -> p k s", s=P)).then_inc(xg_v, 1)
                    dve.wait_ge(sg_done, c + 1)
                    dve.tensor_tensor(hs[:, :], sg[:, :], bank[6][:, 0:DE],
                                      ALU.mult).then_inc(round_link, 1)
                    dve.wait_ge(round_link, 4 * c + 4)
                    dve.tensor_tensor(hs[:, :], hs[:, :], bank[6][:, DE:2 * DE],
                                      ALU.mult).then_inc(bank_free[6], 1)
                    dve.wait_ge(y_ps, 2 * c + 2)
                    dve.tensor_copy(ys[:, HALF:DM], bank[5][:, :]).then_inc(bank_free[5], 1)
            dve.wait_ge(added, dve.value_load(bounds[0:1, NQ:NQ + 1], min_val=NQ, max_val=MAX_ROUNDS))
            norm(1)

        @block.tensor
        def _(pe):
            def low_words(n):
                s = n % NSPL
                return (wh[:, s, :].rearrange("p (k c) -> p k c", k=KC),
                        wl[:, s, :].rearrange("p (k c) -> p k c", k=KC))

            def product(dst, n, ks, high_in, low_in):
                h, l = low_words(n)
                for i, k in enumerate(ks):
                    for w, v in ((h, high_in), (h, low_in), (l, high_in)):
                        mm = pe.matmul(dst, w[:, k, :], v[:, i, :], start=(i == 0 and w is h and v is high_in),
                                       stop=(i == len(ks) - 1 and w is l))
                return mm

            def seed():
                for t in range(TT):
                    for h in range(2):
                        pe.matmul(bank[2 * t + h][:, :], alpha_i[:, :], x1[:, t, h * HALF:(h + 1) * HALF],
                                  start=True, stop=True, skip_group_check=True)

            def attention(i):
                c, stage = i // 3, i % 3
                if stage == 0 and c < CC:
                    if c >= 1:
                        pe.wait_ge(score_sb, 2 * c)
                    for j in range(2):
                        hp = slice(HD * j, HD * (j + 1))
                        pe.matmul(bank[j][:, 0:P], qT[hp, c, 0:P], kT[hp, c, 0:P], start=True, stop=True)
                    for j in range(2):
                        hp = slice(HD * j, HD * (j + 1))
                        pe.matmul(bank[j][:, P:3 * P], qT[hp, c, P:SEQ], kT[hp, c, :],
                                  start=True, stop=True).then_inc(score_ps, 1)
                if stage == 2 and c < CC:
                    if c >= 1:
                        pe.wait_ge(pT_done, 2 * c)
                    for j in range(2):
                        pe.wait_ge(prob_done, 2 * c + j + 1)
                        for b in range(3):
                            mm = pe.transpose(bank[2 + j][:, b * P:(b + 1) * P], sc[:, j, b, :], ident[:, :])
                        mm.then_inc(pT_ps, 1)
                if stage == 0 and 1 <= c <= CC:
                    d = c - 1
                    pe.wait_ge(pT_done, 2 * d + 2)
                    if d >= 2:
                        pe.wait_ge(ol_done, d - 1)
                    for j in range(2):
                        dst = bank[6 + d % 2][HD * j:HD * (j + 1), 0:SEQ]
                        cols = slice((2 * d + j) * HD, (2 * d + j + 1) * HD)
                        pe.matmul(dst, vv[:, 0, cols], pT[:, j, 0:2, :].rearrange("p b q -> p (b q)"),
                                  start=True, stop=False, skip_group_check=True)
                        mm = pe.matmul(dst[:, P:SEQ], vv[:, 1, cols], pT[:, j, 2, :],
                                       start=False, stop=True, skip_group_check=True)
                    mm.then_inc(pv_ps, 1)

            pe.wait_ge(consts, N_CONSTS)
            pe.wait_ge(x_in, 16 * TT)
            for b in range(KC // 2):
                for k in (2 * b, 2 * b + 1):
                    for t in range(TT):
                        mm = pe.transpose(bank[b][:, (k % 2) * SEQ + t * P:(k % 2) * SEQ + (t + 1) * P],
                                          x1[:, t, k::KC], ident[:, :])
                mm.then_inc(xT_ps, 1)
            pe.wait_ge(xl_done, KC // 2)

            for n in range(U0):
                kind, c = unit(n)
                if n >= UA:
                    if n == UA:
                        pe.wait_ge(evac_a, UA)
                    attention(n - UA)
                if n == U0 - 1:
                    pe.wait_ge(score_sb, NH)
                    pe.wait_ge(pT_done, NH)
                    seed()
                pe.wait_ge(lo_done, n + 1)
                if n < 2 * NA:
                    if n >= 2:
                        on_act, count = evacuated(n - 2)
                        pe.wait_ge(evac_a if on_act else evac_v, count)
                    dst = bank[4 + n % 2][:, 0:SEQ]
                else:
                    on_act, count = evacuated(2 * NA - 1 - (n == 2 * NA))
                    if c < 2 and kind == "ga":
                        pe.wait_ge(evac_a if on_act else evac_v, count)
                    half = 0 if kind == "ga" else 1
                    dst = bank[4 + n % 2][:, half * SEQ:(half + 1) * SEQ]
                if kind == "v":
                    h, l = low_words(n)
                    for t in range(TT):
                        for k in range(KC):
                            for v, w in ((xh, h), (xh, l), (xl, h)):
                                mm = pe.matmul(dst[:, t * P:(t + 1) * P], v[:, k, t * P:(t + 1) * P],
                                               w[:, k, :], start=(k == 0 and v is xh and w is h),
                                               stop=(k == KC - 1 and v is xl))
                else:
                    mm = product(dst, n, range(KC), xh, xl)
                mm.then_inc(unit_done, 1)

            def branches(j, m):
                pe.wait_ge(lo_done, UPJ * j + U0 + m + 1)
                product(bank[6 + m][:, 0:SEQ], U0 + m, range(CC), zh, zl)
                product(bank[6 + m][:, SEQ:2 * SEQ], U0 + m, range(CC, KC), oh, ol).then_inc(unit_done, 1)

            def merge(j, m, at):
                n = U0 + at + m
                pe.wait_ge(lo_done, UPJ * j + n + 1)
                pe.wait_ge(yl_done, 2 * j + m + 1)
                s = n % NSPL
                for t in range(TT):
                    for v, w in ((yh, wh), (yh, wl), (yl, wh)):
                        for h in range(2):
                            mm = pe.matmul(bank[2 * t + h][:, :], v[:, m, t * P:(t + 1) * P],
                                           w[:, s, h * HALF:(h + 1) * HALF],
                                           start=False, stop=True, skip_group_check=True)
                mm.then_inc(unit_done, 1)

            pe.wait_ge(ol_done, CC)
            pe.wait_ge(zl_done, CC)
            with pe.Fori(0, JP - 1) as j:
                for m in range(2):
                    branches(j, m)
                pe.wait_ge(sig_done, 2 * j + 2)
                for i in range(2, 6):
                    pe.wait_ge(lo_done, UPJ * j + U0 + i + 1)
                    half = i // 2 - 1
                    product(bank[4 + i % 2][:, half * SEQ:(half + 1) * SEQ], U0 + i, range(KC),
                            xh, xl).then_inc(unit_done, 1)
                for m in range(2):
                    merge(j, m, 6)
            for m in range(2):
                branches(JP - 1, m)
            for m in range(2):
                merge(JP - 1, m, 2)

            pe.wait_ge(y_done, KC)
            for b in range(KC // 2):
                for k in (2 * b, 2 * b + 1):
                    for t in range(TT):
                        pe.wait_ge(x1_done, t + 1)
                        mm = pe.transpose(
                            bank[4 + b][:, (k % 2) * SEQ + t * P:(k % 2) * SEQ + (t + 1) * P],
                            x1[:, t, k::KC], ident[:, :])
                mm.then_inc(x1T_ps, 1)
            for b in bank_free:
                pe.wait_ge(bank_free[b], 1)
            pe.wait_ge(small_in, 80)
            for t in range(TT):
                for k in range(KC):
                    mm = pe.matmul(bank[0][:, t * NL:(t + 1) * NL], x1T[:, k, t * P:(t + 1) * P],
                                   wr[:, k, :], start=(k == 0), stop=(k == KC - 1))
            mm.then_inc(logit_ps, 1)
            pe.wait_ge(routed, 1)
            chosen = rt[:, 9, :, :]
            pe.matmul(bank[1][:, 0:NE], before[:, :], chosen[:, 0, :], start=True, stop=True)
            pe.matmul(bank[1][:, NE:2 * NE], ones[:, :], chosen[:, 0, :], start=True, stop=False)
            pe.matmul(bank[1][:, NE:2 * NE], before[:, :], chosen[:, 1, :], start=False, stop=True)
            for t in range(TT):
                mm = pe.matmul(bank[1][:, TT * NE:(TT + 1) * NE], ones[:, :], chosen[:, t, :],
                               start=(t == 0), stop=(t == TT - 1))
            mm.then_inc(rank_ps, 1)

            pe.wait_ge(rounds_done, 1)
            seed()
            with pe.Fori(0, NQ // 2) as o:
                for half in range(2):
                    q = 2 * o + half
                    w = gu[half]
                    first = pe.value_load(bounds[0:1, bass.ds(q, 1)], min_val=0, max_val=MAX_ROUNDS)
                    end = pe.value_load(bounds[0:1, bass.ds(q + 1, 1)], min_val=1, max_val=MAX_ROUNDS)
                    with pe.Fori(first, end) as c:
                        pe.wait_ge(pick_done, 2 * c + 2)
                        pe.wait_ge(bank_free[4], c + 1)
                        pe.wait_ge(bank_free[5], c + 1)
                        for k in range(KC):
                            for t in range(TT):
                                mm = pe.matmul(bank[4 + k // 4][:, (k % 4) * P:(k % 4 + 1) * P],
                                               x1[:, t, k::KC],
                                               pick[:, t, :, :].rearrange("p e s -> p (e s)"),
                                               start=(t == 0), stop=(t == TT - 1))
                            if k % 4 == 3:
                                mm.then_inc(xg_ps, 1)
                        pe.wait_ge(bank_free[7], c + 1)
                        for t in range(TT):
                            mm = pe.transpose(bank[7][:, SEQ + t * P:SEQ + (t + 1) * P],
                                              pickw[:, t, :, :].rearrange("p e s -> p (e s)"), ident[:, :])
                        mm.then_inc(put_ps, 1)
                        pe.wait_ge(xg_a, c + 1)
                        pe.wait_ge(xg_v, c + 1)
                        pe.wait_ge(bank_free[6], c + 1)
                        pe.wait_ge(gu_in[half], 2 * QE * 16 * (o + 1))
                        for k in range(KC):
                            for e in range(QE):
                                g = slice(SLOTS * e, SLOTS * (e + 1))
                                mm = pe.matmul(bank[6][g, :], xg[:, k, g], w[:, e, k, :],
                                               start=(k == 0), stop=(k == KC - 1))
                        mm.then_inc(gu_ps, 1)
                        pe.wait_ge(bank_free[6], c + 2)
                        pe.wait_ge(put_done, c + 1)
                        for j in range(FC):
                            mm = pe.transpose(bank[7][:, j * P:(j + 1) * P], hs[:, j * P:(j + 1) * P],
                                              ident[:, :])
                        mm.then_inc(hT_ps, 1)
                        pe.wait_ge(bank_free[7], c + 2)
                        pe.wait_ge(dn_in, QE * 16 * (q + 1))
                        for h in range(2):
                            for j in range(FC):
                                for e in range(QE):
                                    g = slice(SLOTS * e, SLOTS * (e + 1))
                                    mm = pe.matmul(bank[4 + h][g, :], hT[:, j, g],
                                                   dn[:, e, j, h * HALF:(h + 1) * HALF],
                                                   start=(j == 0), stop=(j == FC - 1))
                            mm.then_inc(y_ps, 1)
                        pe.wait_ge(bank_free[4], c + 2)
                        pe.wait_ge(bank_free[5], c + 2)
                        for t in range(TT):
                            for h in range(2):
                                mm = pe.matmul(bank[2 * t + h][:, :], put[:, t * P:(t + 1) * P],
                                               ys[:, h * HALF:(h + 1) * HALF],
                                               start=False, stop=True, skip_group_check=True)
                        mm.then_inc(added, 1)
                    pe.drain().then_inc(gu_free[half], 1)
                    pe.drain().then_inc(dn_free, 1)


_INS = ['x', 'w_in', 'conv_w', 'w_out_conv', 'w_out_attn', 'w_o', 'ln1_g', 'ln1_b',
        'w_router_group', 'w_router_expert', 'w_gate', 'w_up', 'w_down', 'ln2_g', 'ln2_b']


def kernel(**inputs):
    import numpy as _np
    import concourse.bacc as _bacc
    from concourse import mybir as _mybir
    from concourse.bass_utils import run_bass_kernel_spmd as _run

    nc = _bacc.Bacc("TRN2", target_bir_lowering=False, num_devices=1)
    arrays, args = {}, []
    for name in _INS:
        a = _np.ascontiguousarray(inputs[name])
        arrays[f"in_{name}"] = a
        args.append(nc.dram_tensor(f"in_{name}", a.shape, _mybir.dt.from_np(a.dtype),
                                   kind="ExternalInput").ap())
    args.append(nc.dram_tensor("out_0", (1, SEQ, DM), _mybir.dt.float32, kind="ExternalOutput").ap())
    hybrid_block(nc, *args)
    r = _run(nc, [arrays], core_ids=[0])
    return r.results[0]["out_0"]
```

```python
import numpy as np
import concourse.bass as bass
from concourse import mybir
from contextlib import ExitStack

F32 = mybir.dt.float32
F32R = mybir.dt.float32r
BF16 = mybir.dt.bfloat16
I32 = mybir.dt.int32
ALU = mybir.AluOpType
ACT = mybir.ActivationFunctionType
AX = mybir.AxisListType

P = 128
SEQ, DM = 256, 1024
TT = SEQ // P
KC = DM // P
CW, AW = 512, 512
CC = CW // P
NH, HD = 8, 64
NG, EPG, DE = 4, 8, 256
NE = NG * EPG
FC = DE // P
QE = 4
NQ = NE // QE
SLOTS = P // QE
NL = NG + NE
EPS = 1e-5
ALPHA = 2.0 ** 0.25
SCALE = HD ** -0.5
MASKED = -1e30
MAX_ROUNDS = NQ + TT * SEQ // SLOTS
N_CONSTS = 10
N_SMALL = 16 * 7
FAR = 1e6
COL_B, COL_C, COL_X, COL_Q, COL_K, COL_V = (CW * i for i in range(6))
COL_GA = 3 * CW + 3 * AW
COL_GB = COL_GA + DM
GRP = 2 * P
NRAW, NSPL = 2, 4
HALF = 512


def hybrid_block(nc, x, w_in, conv_w, w_out_conv, w_out_attn, w_o, ln1_g, ln1_b,
                 w_router_group, w_router_expert, w_gate, w_up, w_down, ln2_g, ln2_b, out):
    x_v = x[0, :, :].rearrange("(t p) d -> p t d", p=P)
    out_v = out[0, :, :].rearrange("(t p) d -> p t d", p=P)
    win_v = w_in[0, :, :].rearrange("(p k) c -> p k c", k=KC)
    wc_v = w_out_conv[0, :, :].rearrange("(j p) d -> p j d", p=P)
    wa_v = w_out_attn[0, :, :].rearrange("(j p) d -> p j d", p=P)
    wo_v = w_o[0, :, :].rearrange("(j p) d -> p j d", p=P)
    convw_v = conv_w[0, :, :].rearrange("i (j p) -> p j i", p=P)
    gcol_v = ln1_g[0, :].rearrange("(p k) -> p k", k=KC)
    bcol_v = ln1_b[0, :].rearrange("(p k) -> p k", k=KC)
    wrg_v = w_router_group[0, :, :].rearrange("(p k) g -> p k g", k=KC)
    wre_v = w_router_expert[0, :, :].rearrange("(p k) e -> p k e", k=KC)
    wg_v = w_gate[0, :, :, :].rearrange("e (p k) f -> p e k f", k=KC)
    wu_v = w_up[0, :, :, :].rearrange("e (p k) f -> p e k f", k=KC)
    wd_v = w_down[0, :, :, :].rearrange("e (j p) d -> p e j d", p=P)

    ctx = ExitStack()
    with ctx:
        def sb(name, shape, dt=F32, where=ctx):
            return where.enter_context(nc.sbuf_tensor(name, shape, dt))

        def sem(name):
            return ctx.enter_context(nc.semaphore(name))

        x1 = sb("x1", [P, TT, DM])
        wr = sb("wr", [P, KC, NL])
        convw = sb("convw", [P, CC, 3])
        ident = sb("ident", [P, P])
        alpha_i = sb("alpha_i", [P, P])
        before = sb("before", [P, P], BF16)
        ones_b = sb("ones_b", [P, P], BF16)
        ones = sb("ones", [P, P])
        gcol = sb("gcol", [P, KC])
        bcol = sb("bcol", [P, KC])
        wrb = sb("wrb", [P, KC, NL])
        rbias = sb("rbias", [P, NL])
        chosen = sb("chosen", [P, TT, NE], BF16)
        slot_id = sb("slot_id", [P, SLOTS])
        group_key = sb("group_key", [P, NG])
        expert_key = sb("expert_key", [P, NE])
        half_neg = sb("half_neg", [P, TT])
        stats = sb("stats", [P, TT, 2, 6])
        moments = sb("moments", [P, TT, 2])
        rstd = sb("rstd", [P, TT])
        shift = sb("shift", [P, TT])
        rt = sb("rt", [P, 13, TT, NL])
        rs = sb("rs", [P, 16, TT])
        rounds_f = sb("rounds_f", [P, 4, 16])
        rounds_i = sb("rounds_i", [P, 1, 16], I32)
        bounds = sb("bounds", [P, 16], I32)
        rank = sb("rank", [P, TT, NE])
        comb = sb("comb", [P, TT, NE])

        gu0 = sb("gu0", [P, QE, KC, 2 * DE])
        dn_scope = ExitStack()
        qT = sb("qT", [P, CC, SEQ], where=dn_scope)
        kT = sb("kT", [P, CC, SEQ], where=dn_scope)
        vv = sb("vv", [P, TT, AW], where=dn_scope)
        dist = sb("dist", [P, 3, P], where=dn_scope)
        sc = sb("sc", [P, 2, 3, P], where=dn_scope)
        pT = sb("pT", [P, 2, 3, P], where=dn_scope)
        nmax = sb("nmax", [P, 2, 2], where=dn_scope)
        rsum = sb("rsum", [P, 2, 2], where=dn_scope)
        rinv = sb("rinv", [P, 2, 2], where=dn_scope)
        cc_t = sb("cc_t", [P, 2, SEQ], where=dn_scope)
        u_t = sb("u_t", [P, 2, 2 + SEQ], where=dn_scope)
        cv_t = sb("cv_t", [P, 2, SEQ], where=dn_scope)
        z_t = sb("z_t", [P, SEQ], where=dn_scope)
        dn_scope.close()
        dn = sb("dn", [P, QE, FC, DM])

        mix_scope = ExitStack()
        xh = sb("xh", [P, KC, SEQ], F32R, mix_scope)
        xl = sb("xl", [P, KC, SEQ], F32R, mix_scope)
        raw = sb("raw", [P, NRAW, KC * GRP], where=mix_scope)
        wh = sb("wh", [P, NSPL, KC * P], F32R, mix_scope)
        wl = sb("wl", [P, NSPL, KC * P], F32R, mix_scope)
        zh = sb("zh", [P, CC, SEQ], F32R, mix_scope)
        zl = sb("zl", [P, CC, SEQ], F32R, mix_scope)
        oh = sb("oh", [P, CC, SEQ], F32R, mix_scope)
        ol = sb("ol", [P, CC, SEQ], F32R, mix_scope)
        yh = sb("yh", [P, 2, SEQ], F32R, mix_scope)
        yl = sb("yl", [P, 2, SEQ], F32R, mix_scope)
        sig = sb("sig", [P, 2, 2 * SEQ], where=mix_scope)
        yt = sb("yt", [P, 2, SEQ], where=mix_scope)
        mix_scope.close()
        lng = sb("lng", [P, DM])
        lnb = sb("lnb", [P, DM])
        gu1 = sb("gu1", [P, QE, KC, 2 * DE])
        x1T = sb("x1T", [P, KC, SEQ])
        xg = sb("xg", [P, KC, P])
        pick = sb("pick", [P, TT, QE, SLOTS])
        pickw = sb("pickw", [P, TT, QE, SLOTS])
        put = sb("put", [P, SEQ])
        sg = sb("sg", [P, DE])
        hs = sb("hs", [P, DE])
        hT = sb("hT", [P, FC, P])
        ys = sb("ys", [P, DM])

        bank = [ctx.enter_context(nc.psum_tensor(f"bank{i}", [P, HALF], F32)) for i in range(8)]

        gu = [gu0, gu1]
        e_in, e_out = (rt[:, i, :, 0:NG + 1] for i in (11, 12))

        x_in = sem("x_in")
        small_in = sem("small_in")
        raw_in = [sem(f"raw_in{i}") for i in range(NRAW)]
        ln_in = sem("ln_in")
        gu_in = [sem(f"gu_in{i}") for i in range(2)]
        dn_in = [sem(f"dn_in{i}") for i in range(2)]
        out_done = sem("out_done")
        zeroed = sem("zeroed")
        ident_done = sem("ident_done")
        consts = sem("consts")
        pool_link = sem("pool_link")
        xT_ps = sem("xT_ps")
        xh_done = sem("xh_done")
        xl_done = sem("xl_done")
        hi_done = sem("hi_done")
        lo_done = sem("lo_done")
        unit_done = sem("unit_done")
        evac_a = sem("evac_a")
        evac_v = sem("evac_v")
        score_ps = sem("score_ps")
        score_sb = sem("score_sb")
        exp_done = sem("exp_done")
        prob_done = sem("prob_done")
        pT_ps = sem("pT_ps")
        pT_done = sem("pT_done")
        pv_ps = sem("pv_ps")
        oh_done = sem("oh_done")
        ol_done = sem("ol_done")
        z_done = sem("z_done")
        zh_done = sem("zh_done")
        zl_done = sem("zl_done")
        sig_done = sem("sig_done")
        y_done = sem("y_done")
        yh_done = sem("yh_done")
        yl_done = sem("yl_done")
        dve_link = sem("dve_link")
        nmax_done = sem("nmax_done")
        moment_done = sem("moment_done")
        rstd_done = sem("rstd_done")
        shift_done = sem("shift_done")
        norm_done = sem("norm_done")
        acc_done = sem("acc_done")
        wrb_done = sem("wrb_done")
        bias_ps = sem("bias_ps")
        bias_read = sem("bias_read")
        x1_done = sem("x1_done")
        x1T_ps = sem("x1T_ps")
        logit_ps = sem("logit_ps")
        gexp_in = sem("gexp_in")
        gexp_done = sem("gexp_done")
        routed = sem("routed")
        rank_ps = sem("rank_ps")
        rounds_done = sem("rounds_done")
        y_link = sem("y_link")
        round_link = sem("round_link")
        bank_free = {b: sem(f"bank_free{b}") for b in (4, 5, 6, 7)}
        pick_done = sem("pick_done")
        xg_ps = sem("xg_ps")
        xg_a = sem("xg_a")
        xg_v = sem("xg_v")
        put_ps = sem("put_ps")
        put_done = sem("put_done")
        gu_ps = sem("gu_ps")
        sg_done = sem("sg_done")
        h_done = sem("h_done")
        hT_ps = sem("hT_ps")
        hT_done = sem("hT_done")
        y_ps = sem("y_ps")
        ys_a = sem("ys_a")
        ys_v = sem("ys_v")
        added = sem("added")

        phase_a = ([("q", 0), ("q", 1), ("k", 0), ("k", 1), ("v", 0), ("v", 1)]
                   + [(n, c) for c in range(CC // 2) for n in ("cc", "cx", "cb")])
        lead = [("ga", 0), ("gb", 0)]
        NA = len(phase_a)
        PB = NA + len(lead)
        JP = KC // 2
        START = {"q": COL_Q, "k": COL_K, "v": COL_V, "cc": COL_C, "cx": COL_X, "cb": COL_B,
                 "ga": COL_GA, "gb": COL_GB}

        sequence = (phase_a + lead
                    + [x for j in range(JP - 1) for x in (("ca", j), ("ga", j + 1), ("gb", j + 1), ("wo", j))]
                    + [("ca", JP - 1), ("wo", JP - 1)])
        UNITS = 2 * len(sequence)
        U0 = 2 * PB
        UPJ = 8
        UA = 12
        assert U0 % NSPL == 0 and PB % NRAW == 0 and UPJ % NSPL == 0

        def unit(n):
            return sequence[n // 2][0], 2 * sequence[n // 2][1] + n % 2

        def evacuated(n):
            mine = ("q", "k", "v", "cc")
            on_act = unit(n)[0] in mine
            return on_act, sum((unit(m)[0] in mine) == on_act for m in range(n + 1))

        block = ctx.enter_context(nc.Block())

        @block.sync
        def _(sp):
            def load_pair(slot, kind, idx):
                s = raw_in[slot]
                dst = raw[:, slot, :].rearrange("p (k c) -> p k c", k=KC)
                if kind in START:
                    for k in (0, KC // 2):
                        sp.dma_start(dst[:, k:k + KC // 2, :],
                                     win_v[:, k:k + KC // 2, bass.ds(idx * GRP + START[kind], GRP)]
                                     ).then_inc(s, 16)
                elif kind == "ca":
                    sp.dma_start(dst[:, 0:CC, :], wc_v[:, :, bass.ds(idx * GRP, GRP)]).then_inc(s, 16)
                    sp.dma_start(dst[:, CC:KC, :], wa_v[:, :, bass.ds(idx * GRP, GRP)]).then_inc(s, 16)
                else:
                    for i in range(2):
                        sp.dma_start(dst[:, :, i * P:(i + 1) * P],
                                     wo_v[:, bass.ds(idx * 2 + i, 1), :].rearrange(
                                         "p a (k c) -> p (a k) c", k=KC)).then_inc(s, 16)

            def load_gu(h, q, experts):
                for e in experts:
                    for c, src in ((0, wg_v), (DE, wu_v)):
                        sp.dma_start(gu[h][:, e, :, c:c + DE],
                                     src[:, bass.ds(q * QE + e, 1), :, :]).then_inc(gu_in[h], 16)

            def load_dn(q):
                for h in range(2):
                    for e in range(QE):
                        sp.dma_start(dn[:, e, :, h * HALF:(h + 1) * HALF],
                                     wd_v[:, bass.ds(q * QE + e, 1), :, h * HALF:(h + 1) * HALF]
                                     ).then_inc(dn_in[h], 16)

            for t in range(TT):
                sp.dma_start(x1[:, t, :], x_v[:, t, :]).then_inc(x_in, 16)
            ahead = [(e, c, k) for e in range(QE) for c in range(2) for k in range(2)]
            for n in range(PB):
                if n >= NRAW:
                    sp.wait_ge(lo_done, 2 * (n - NRAW + 1))
                load_pair(n % NRAW, *sequence[n])
                if n == 1:
                    for dst, src in ((wr[:, :, 0:NG], wrg_v), (wr[:, :, NG:NL], wre_v),
                                     (gcol[:, :], gcol_v), (bcol[:, :], bcol_v),
                                     (convw[:, :, 0], convw_v[:, :, 0]), (convw[:, :, 1], convw_v[:, :, 1]),
                                     (convw[:, :, 2], convw_v[:, :, 2])):
                        sp.dma_start(dst, src, allow_slow_non_contiguous=True).then_inc(small_in, 16)
                for _ in range(0 if n < NRAW else 2 if n % 3 == 0 else 1):
                    if ahead:
                        e, c, k = ahead.pop(0)
                        ks = slice(k * KC // 2, (k + 1) * KC // 2)
                        sp.dma_start(gu0[:, e, ks, c * DE:(c + 1) * DE],
                                     (wg_v, wu_v)[c][:, e, ks, :]).then_inc(gu_in[0], 16)
            assert not ahead
            with sp.Fori(0, JP - 1) as j:
                for i, (kind, idx) in enumerate((("ca", j), ("ga", j + 1), ("gb", j + 1), ("wo", j))):
                    sp.wait_ge(lo_done, UPJ * j + 2 * (PB + i - NRAW + 1))
                    load_pair((PB + i) % NRAW, kind, idx)
            for n in range(len(sequence) - 2, len(sequence)):
                sp.wait_ge(lo_done, 2 * (n - NRAW + 1))
                load_pair(n % NRAW, *sequence[n])
            sp.wait_ge(pv_ps, CC)
            sp.wait_ge(zl_done, CC)
            load_dn(0)
            sp.wait_ge(acc_done, TT)
            load_gu(1, 1, range(QE))

            sp.wait_ge(rounds_done, 1)

            def through(q):
                return sp.value_load(bounds[0:1, bass.ds(q, 1)], min_val=1, max_val=MAX_ROUNDS)

            with sp.Fori(1, NQ // 2) as o:
                for h in range(2):
                    q = 2 * o + h
                    sp.wait_ge(gu_ps, through(q - 1))
                    load_gu(h, q, (0, 1))
                    sp.wait_ge(y_ps, 2 * through(q - 1))
                    load_dn(q - 1)
                    load_gu(h, q, (2, 3))
            sp.wait_ge(y_ps, 2 * through(NQ - 1))
            load_dn(NQ - 1)
            for t in range(TT):
                for h in range(2):
                    cols = slice(h * HALF, (h + 1) * HALF)
                    sp.wait_ge(x1_done, TT + 2 * t + h + 1)
                    sp.dma_start(out_v[:, t, cols], x1[:, t, cols]).then_inc(out_done, 16)
            sp.wait_ge(out_done, 16 * 2 * TT)

        @block.gpsimd
        def _(pool):
            linked = [0]

            def link(ins):
                linked[0] += 1
                ins.then_inc(pool_link, 1)
                pool.wait_ge(pool_link, linked[0])

            def const(ins):
                ins.then_inc(consts, 1)

            link(pool.memset(ident[:, :], 0.0))
            pool.affine_select(out=ident[:, :], in_=ident[:, :], compare_op=ALU.not_equal, fill=1.0,
                               base=0, pattern=[[-1, P]], channel_multiplier=1).then_inc(ident_done, 1)
            link(pool.iota(dist[:, 0, :], pattern=[[1, P]], base=0, channel_multiplier=-1,
                           allow_small_or_imprecise_dtypes=True))
            link(pool.affine_select(out=dist[:, 0, :], in_=dist[:, 0, :], compare_op=ALU.is_ge,
                                    fill=MASKED, base=0, pattern=[[-1, P]], channel_multiplier=1))
            const(pool.iota(dist[:, 1, :], pattern=[[1, P]], base=-P, channel_multiplier=-1,
                            allow_small_or_imprecise_dtypes=True))
            const(pool.tensor_copy(dist[:, 2, :], dist[:, 0, :]))
            link(pool.memset(alpha_i[:, :], 0.0))
            const(pool.affine_select(out=alpha_i[:, :], in_=alpha_i[:, :], compare_op=ALU.not_equal,
                                     fill=ALPHA, base=0, pattern=[[-1, P]], channel_multiplier=1))
            link(pool.memset(before[:, :], 1.0))
            const(pool.affine_select(out=before[:, :], in_=before[:, :], compare_op=ALU.is_gt, fill=0.0,
                                     base=0, pattern=[[1, P]], channel_multiplier=-1))
            const(pool.memset(ones[:, :], 1.0))
            const(pool.memset(ones_b[:, :], 1.0))
            const(pool.iota(slot_id[:, :], pattern=[[1, SLOTS]], base=0, channel_multiplier=0,
                            allow_small_or_imprecise_dtypes=True))
            const(pool.iota(group_key[:, :], pattern=[[-1, NG]], base=NG, channel_multiplier=0,
                            allow_small_or_imprecise_dtypes=True))
            const(pool.iota(expert_key[:, :], pattern=[[-1, NE]], base=NE, channel_multiplier=0,
                            allow_small_or_imprecise_dtypes=True))
            const(pool.memset(half_neg[:, :], -0.5))
            pool.wait_ge(consts, N_CONSTS)
            for n, (g, b) in enumerate(((ln1_g, ln1_b), (ln2_g, ln2_b))):
                if n == 0:
                    pool.wait_ge(unit_done, UNITS - 6)
                else:
                    pool.wait_ge(x1_done, TT)
                pool.dma_start(lng[:, :], g[0:1, :].broadcast_to([P, DM])).then_inc(ln_in, 16)
                pool.dma_start(lnb[:, :], b[0:1, :].broadcast_to([P, DM])).then_inc(ln_in, 16)
                for t in range(TT):
                    pool.wait_ge(moment_done, TT * n + t + 1)
                    pool.tensor_tensor(rstd[:, t:t + 1], moments[:, t, 1:2], half_neg[:, 0:1],
                                       ALU.pow).then_inc(rstd_done, 1)

        @block.scalar
        def _(act):
            def high(n, j=None):
                pair, s, more = n // 2, n % NSPL, 0 if j is None else j
                if n % 2 == 0:
                    act.wait_ge(raw_in[pair % NRAW], more * 16 * UPJ // NRAW + 32 * (pair // NRAW + 1))
                if n >= NSPL:
                    by_pair = n % 2 == 0 and unit(n - NSPL)[0] == "v"
                    act.wait_ge(unit_done, more * UPJ + n - NSPL + 1 + by_pair)
                act.activation(wh[:, s, :].rearrange("p (k c) -> p k c", k=KC),
                               raw[:, pair % NRAW, :].rearrange("p (k c) -> p k c", k=KC)
                               [:, :, n % 2 * P:(n % 2 + 1) * P], ACT.Copy).then_inc(hi_done, 1)

            def attention(i):
                c = i // 3
                if i % 3 == 0 and 1 <= c <= CC:
                    for j in range(2):
                        act.wait_ge(pT_ps, 2 * (c - 1) + j + 1)
                        if c >= 2:
                            act.wait_ge(pv_ps, c - 1)
                        act.activation(pT[:, j, :, :],
                                       bank[2 + j][:, 0:3 * P].rearrange("p (b q) -> p b q", b=3),
                                       ACT.Copy).then_inc(pT_done, 1)
                if i % 3 == 0 and c < CC:
                    for j in range(2):
                        act.wait_ge(nmax_done, 2 * c + j + 1)
                        act.activation(sc[:, j, 0, :], sc[:, j, 0, :], ACT.Exp, bias=nmax[:, j, 0:1],
                                       accum_out=rsum[:, j, 0:1])
                        act.activation(sc[:, j, 1:3, :], sc[:, j, 1:3, :], ACT.Exp,
                                       bias=nmax[:, j, 1:2], accum_out=rsum[:, j, 1:2]
                                       ).then_inc(exp_done, 1)
                if i % 3 == 2 and 1 <= c <= CC:
                    act.wait_ge(pv_ps, c)
                    act.activation(oh[:, c - 1, :], bank[6 + (c - 1) % 2][:, 0:SEQ],
                                   ACT.Copy).then_inc(oh_done, 1)

            for b in range(KC // 2):
                act.wait_ge(xT_ps, b + 1)
                act.activation(xh[:, 2 * b:2 * b + 2, :],
                               bank[b][:, :].rearrange("p (k s) -> p k s", k=2),
                               ACT.Copy).then_inc(xh_done, 1)
            for n in range(NSPL):
                high(n)

            for n in range(U0):
                kind, c = unit(n)
                src = bank[4 + n % 2][:, 0:SEQ]
                if n >= UA:
                    attention(n - UA)
                if kind in ("q", "k", "v", "cc"):
                    act.wait_ge(unit_done, n + 1)
                if kind == "q":
                    act.activation(qT[:, c, :], src, ACT.Copy, scale=SCALE).then_inc(evac_a, 1)
                elif kind == "k":
                    act.activation(kT[:, c, :], src, ACT.Copy).then_inc(evac_a, 1)
                elif kind == "v":
                    act.activation(vv[:, n % 2, c // 2 * GRP:(c // 2 + 1) * GRP], src,
                                   ACT.Copy).then_inc(evac_a, 1)
                elif kind == "cc":
                    if c >= 2:
                        act.wait_ge(evac_v, evacuated(n - 4)[1])
                    act.activation(cc_t[:, c % 2, :], src, ACT.Copy).then_inc(evac_a, 1)
                high(n + NSPL)
                if kind == "cb":
                    act.wait_ge(z_done, c + 1)
                    act.activation(zh[:, c, :], z_t[:, :], ACT.Copy).then_inc(zh_done, 1)

            def gates():
                for m in range(2):
                    act.activation(sig[:, m, :], bank[4 + m][:, :], ACT.Sigmoid).then_inc(sig_done, 1)

            def y_high(j, m):
                act.wait_ge(y_done, 2 * j + m + 1)
                act.activation(yh[:, m, :], yt[:, m, :], ACT.Copy).then_inc(yh_done, 1)

            act.wait_ge(unit_done, U0)
            gates()
            with act.Fori(0, JP - 1) as j:
                for i in range(UPJ):
                    high(U0 + i + NSPL, j)
                    if i in (1, 2):
                        y_high(j, i - 1)
                    if i == 5:
                        act.wait_ge(unit_done, UPJ * j + U0 + 6)
                        gates()
            for m in range(2):
                y_high(JP - 1, m)

            for t in range(TT):
                act.wait_ge(shift_done, t + 1)
                for h in range(2):
                    act.activation(x1[:, t, h * HALF:(h + 1) * HALF], bank[2 * t + h][:, :],
                                   ACT.Identity, scale=rstd[:, t:t + 1],
                                   bias=shift[:, t:t + 1]).then_inc(norm_done, 1)
            for t in range(TT):
                for g in range(2):
                    b = 4 + 2 * t + g
                    act.wait_ge(x1T_ps, b - 3)
                    act.activation(x1T[:, g * KC // 2:(g + 1) * KC // 2, t * P:(t + 1) * P],
                                   bank[b][:, :].rearrange("p (k s) -> p k s", s=P),
                                   ACT.Copy).then_inc(bank_free[b], 1)
            act.wait_ge(gexp_in, 1)
            act.activation(e_out, e_in, ACT.Exp).then_inc(gexp_done, 1)

            act.wait_ge(rounds_done, 1)
            with act.Fori(0, act.value_load(bounds[0:1, NQ:NQ + 1], min_val=NQ, max_val=MAX_ROUNDS)) as c:
                act.wait_ge(xg_ps, 2 * c + 1)
                act.activation(xg[:, 0:KC // 2, :], bank[4][:, :].rearrange("p (k s) -> p k s", s=P),
                               ACT.Copy).then_inc(xg_a, 1)
                act.wait_ge(put_ps, c + 1)
                act.activation(put[:, :], bank[7][:, SEQ:2 * SEQ], ACT.Copy).then_inc(put_done, 1)
                act.wait_ge(gu_ps, c + 1)
                act.activation(sg[:, :], bank[6][:, 0:DE], ACT.Sigmoid).then_inc(sg_done, 1)
                act.wait_ge(hT_ps, c + 1)
                act.activation(hT[:, :, :], bank[7][:, 0:SEQ].rearrange("p (j s) -> p j s", j=FC),
                               ACT.Copy).then_inc(bank_free[7], 1)
                act.wait_ge(y_ps, 2 * c + 1)
                act.activation(ys[:, 0:HALF], bank[4][:, :], ACT.Copy).then_inc(bank_free[4], 1)

        @block.vector
        def _(dve):
            linked = [0]

            def link(ins):
                linked[0] += 1
                ins.then_inc(dve_link, 1)
                dve.wait_ge(dve_link, linked[0])

            def low(n, j=None):
                pair, s, more = n // 2, n % NSPL, 0 if j is None else j
                dve.wait_ge(hi_done, more * UPJ + n + 1)
                dve.tensor_tensor(wl[:, s, :].rearrange("p (k c) -> p k c", k=KC),
                                  raw[:, pair % NRAW, :].rearrange("p (k c) -> p k c", k=KC)
                                  [:, :, n % 2 * P:(n % 2 + 1) * P],
                                  wh[:, s, :].bitcast(F32).rearrange("p (k c) -> p k c", k=KC),
                                  ALU.subtract).then_inc(lo_done, 1)

            def attention(i):
                c = i // 3
                if i % 3 == 0 and c < CC:
                    for j in range(2):
                        dve.wait_ge(score_ps, 2 * c + j + 1)
                        if c >= 1:
                            dve.wait_ge(pT_ps, 2 * c)
                        dve.scalar_tensor_tensor(
                            sc[:, j, :, :], dist[:, :, :], float(2.0 ** (-8.0 * (2 * c + j + 1) / NH)),
                            bank[j][:, 0:3 * P].rearrange("p (b k) -> p b k", b=3),
                            ALU.mult, ALU.add).then_inc(score_sb, 1)
                    for j in range(2):
                        dve.wait_ge(score_sb, 2 * c + j + 1)
                        dve.tensor_reduce(nmax[:, j, 0:1], sc[:, j, 0, :], AX.X, ALU.max, negate=True)
                        dve.tensor_reduce(nmax[:, j, 1:2], sc[:, j, 1:3, :], AX.XY, ALU.max,
                                          negate=True).then_inc(nmax_done, 1)
                if i % 3 == 1 and c < CC:
                    dve.wait_ge(exp_done, 2 * c + 2)
                    link(dve.reciprocal(rinv[:, :, :], rsum[:, :, :]))
                    for j in range(2):
                        dve.tensor_scalar(sc[:, j, 0, :], sc[:, j, 0, :], rinv[:, j, 0:1], None, ALU.mult)
                        dve.tensor_scalar(sc[:, j, 1:3, :], sc[:, j, 1:3, :], rinv[:, j, 1:2], None,
                                          ALU.mult).then_inc(prob_done, 1)
                if i % 3 == 2 and 1 <= c <= CC:
                    dve.wait_ge(oh_done, c)
                    dve.tensor_tensor(ol[:, c - 1, :], bank[6 + (c - 1) % 2][:, 0:SEQ],
                                      oh[:, c - 1, :].bitcast(F32), ALU.subtract).then_inc(ol_done, 1)

            link(dve.memset(u_t[:, :, 0:2], 0.0))
            for b in range(KC // 2):
                dve.wait_ge(xh_done, b + 1)
                dve.tensor_tensor(xl[:, 2 * b:2 * b + 2, :],
                                  bank[b][:, :].rearrange("p (k s) -> p k s", k=2),
                                  xh[:, 2 * b:2 * b + 2, :].bitcast(F32),
                                  ALU.subtract).then_inc(xl_done, 1)
            for n in range(NSPL):
                low(n)
            dve.wait_ge(consts, N_CONSTS)
            dve.wait_ge(small_in, N_SMALL)
            gb, bb = (v[:, :].unsqueeze(2).to_broadcast([P, KC, NL]) for v in (gcol, bcol))
            link(dve.tensor_tensor(wrb[:, :, :], wr[:, :, :], bb, ALU.mult))
            dve.tensor_tensor(wr[:, :, :], wr[:, :, :], gb, ALU.mult).then_inc(wrb_done, 1)
            for n in range(U0):
                kind, c = unit(n)
                src = bank[4 + n % 2][:, 0:SEQ]
                u, cv = u_t[:, c % 2, :], cv_t[:, c % 2, :]
                if n >= UA:
                    attention(n - UA)
                if kind == "cx":
                    dve.wait_ge(unit_done, n + 1)
                    dve.wait_ge(evac_a, evacuated(n - 2)[1])
                    dve.tensor_tensor(u[:, 2:], src, cc_t[:, c % 2, :], ALU.mult).then_inc(evac_v, 1)
                if kind == "cb":
                    dve.wait_ge(unit_done, n + 1)
                    dve.tensor_tensor(z_t[:, :], src, cv, ALU.mult).then_inc(evac_v, 1)
                    dve.wait_ge(evac_v, evacuated(n)[1])
                    dve.engine_nop().then_inc(z_done, 1)
                low(n + NSPL)
                if kind == "cx":
                    dve.wait_ge(evac_v, evacuated(n)[1])
                    link(dve.tensor_scalar(cv, u[:, 2:], convw[:, c, 2:3], None, ALU.mult))
                    link(dve.scalar_tensor_tensor(cv, u[:, 1:1 + SEQ], convw[:, c, 1:2], cv,
                                                  ALU.mult, ALU.add))
                    link(dve.scalar_tensor_tensor(cv, u[:, 0:SEQ], convw[:, c, 0:1], cv,
                                                  ALU.mult, ALU.add))
                if kind == "cb":
                    dve.wait_ge(zh_done, c + 1)
                    dve.tensor_tensor(zl[:, c, :], z_t[:, :], zh[:, c, :].bitcast(F32),
                                      ALU.subtract).then_inc(zl_done, 1)
                    dve.wait_ge(zl_done, c + 1)
                if n == 2:
                    dve.wait_ge(bias_ps, 1)
                    dve.tensor_copy(rbias[:, :], bank[6][:, 0:NL]).then_inc(bias_read, 1)

            def y_chunk(j, m):
                dve.wait_ge(unit_done, UPJ * j + U0 + m + 1)
                dve.wait_ge(sig_done, 2 * j + m + 1)
                dve.tensor_tensor(sig[:, m, :], sig[:, m, :], bank[6 + m][:, :],
                                  ALU.mult).then_inc(y_link, 1)
                dve.wait_ge(y_link, 2 * j + m + 1)
                dve.tensor_tensor(yt[:, m, :], sig[:, m, 0:SEQ], sig[:, m, SEQ:2 * SEQ],
                                  ALU.add).then_inc(y_done, 1)

            def y_low(j, m):
                dve.wait_ge(yh_done, 2 * j + m + 1)
                dve.tensor_tensor(yl[:, m, :], yt[:, m, :], yh[:, m, :].bitcast(F32),
                                  ALU.subtract).then_inc(yl_done, 1)

            with dve.Fori(0, JP - 1) as j:
                for i in range(UPJ):
                    if i < 2:
                        y_chunk(j, i)
                    low(U0 + i + NSPL, j)
                    if i in (2, 3):
                        y_low(j, i - 2)
            for m in range(2):
                y_chunk(JP - 1, m)
            for m in range(2):
                y_low(JP - 1, m)

            def variance(t):
                link(dve.bn_aggr(moments[:, t, :], stats[:, t, :, :]))
                dve.tensor_scalar(moments[:, t, 1:2], moments[:, t, 1:2], EPS, None,
                                  ALU.add).then_inc(moment_done, 1)

            for t in range(TT):
                dve.wait_ge(acc_done, t + 1)
                dve.bn_stats(stats[:, t, 0, :], bank[2 * t][:, :])
                link(dve.bn_stats(stats[:, t, 1, :], bank[2 * t + 1][:, :]))
                variance(t)
            for t in range(TT):
                dve.wait_ge(rstd_done, t + 1)
                dve.scalar_tensor_tensor(shift[:, t:t + 1], moments[:, t, 0:1], -1.0, rstd[:, t:t + 1],
                                         ALU.mult, ALU.mult).then_inc(shift_done, 1)
            dve.wait_ge(ln_in, 32)
            for t in range(TT):
                dve.wait_ge(x1T_ps, 2 * t + 2)
                link(dve.tensor_tensor(x1[:, t, :], x1[:, t, :], lng[:, :], ALU.mult))
                dve.tensor_tensor(x1[:, t, :], x1[:, t, :], lnb[:, :], ALU.add).then_inc(x1_done, 1)

            def over(v, n):
                return v.unsqueeze(2).to_broadcast([P, TT, n])

            def first_max(v, key, n, top, eq, hot, scratch):
                link(dve.tensor_reduce(top, v, AX.X, ALU.max))
                for t in range(TT):
                    ins = dve.scalar_tensor_tensor(eq[:, t, :], v[:, t, :], top[:, t:t + 1], key,
                                                   ALU.is_ge, ALU.mult)
                link(ins)
                link(dve.tensor_reduce(scratch, eq, AX.X, ALU.max))
                link(dve.tensor_tensor(hot, eq, over(scratch, n), ALU.is_equal))

            logit = rt[:, 0, :, :]
            gl, el = logit[:, :, 0:NG], logit[:, :, NG:NL]
            eq, masked, hot1, hot2, part = (rt[:, i, :, 0:NE] for i in range(1, 6))
            geq, ghot, pen = (rt[:, i, :, 0:NG] for i in range(6, 9))
            gtop, top1, top2, tmp, gsum, w1, w2 = (rs[:, i, :] for i in range(7))
            link(dve.memset(rounds_f[:, :, :], 0.0))
            dve.wait_ge(logit_ps, 1)
            link(dve.tensor_tensor(logit, bank[4][:, 0:TT * NL].rearrange("p (t n) -> p t n", t=TT),
                                   rbias[:, :].unsqueeze(1).to_broadcast([P, TT, NL]), ALU.add))
            first_max(gl, group_key[:, :], NG, gtop, geq, ghot, tmp)
            link(dve.tensor_scalar(pen, ghot, -MASKED, MASKED, ALU.mult, ALU.add))
            link(dve.tensor_tensor(masked.rearrange("p t (g e) -> p t g e", g=NG),
                                   el.rearrange("p t (g e) -> p t g e", g=NG),
                                   pen.unsqueeze(3).to_broadcast([P, TT, NG, EPG]), ALU.add))
            first_max(masked, expert_key[:, :], NE, top1, eq, hot1, tmp)
            link(dve.scalar_tensor_tensor(masked, hot1, 100.0 * MASKED, masked, ALU.mult, ALU.add))
            first_max(masked, expert_key[:, :], NE, top2, eq, hot2, tmp)
            dve.tensor_tensor(chosen[:, :, :], hot1, hot2, ALU.add).then_inc(routed, 1)
            dve.tensor_tensor(e_in[:, :, 0:NG], gl, over(gtop, NG), ALU.subtract)
            dve.tensor_tensor(e_in[:, :, NG], top2, top1, ALU.subtract).then_inc(gexp_in, 1)
            dve.wait_ge(rank_ps, 1)
            counts = bank[5][0:1, TT * NE:(TT + 1) * NE].rearrange("p (q e) -> p q e", q=NQ)
            rf, ri = rounds_f[0:1, :, :], rounds_i[0:1, 0, 0:NQ]
            link(dve.tensor_reduce(rf[:, 0, NQ:2 * NQ], counts, AX.X, ALU.max))
            link(dve.tensor_scalar(ri, rf[:, 0, NQ:2 * NQ], float(SLOTS - 1), None, ALU.add))
            link(dve.tensor_scalar(ri, ri, SLOTS.bit_length() - 1, None, ALU.logical_shift_right))
            link(dve.tensor_scalar(rf[:, 0, NQ:2 * NQ], ri, 1.0, None, ALU.max))
            for i in range(3):
                d = 1 << i
                link(dve.tensor_tensor(rf[:, i + 1, NQ:2 * NQ], rf[:, i, NQ:2 * NQ],
                                       rf[:, i, NQ - d:2 * NQ - d], ALU.add))
            dve.tensor_copy(bounds[0:1, 0:NQ + 1], rf[:, 3, NQ - 1:2 * NQ]).then_inc(rounds_done, 1)
            ranks = bank[5][:, 0:TT * NE].rearrange("p (t n) -> p t n", t=TT)
            link(dve.scalar_tensor_tensor(rank[:, :, :], ranks, FAR, chosen[:, :, :], ALU.add, ALU.mult))
            link(dve.tensor_scalar(rank[:, :, :], rank[:, :, :], -FAR, None, ALU.add))
            dve.wait_ge(gexp_done, 1)
            link(dve.tensor_reduce(gsum, e_out[:, :, 0:NG], AX.X, ALU.add))
            link(dve.scalar_tensor_tensor(w1, e_out[:, :, NG], 1.0, gsum, ALU.add, ALU.mult))
            link(dve.reciprocal(w1, w1))
            link(dve.tensor_tensor(w2, w1, e_out[:, :, NG], ALU.mult))
            dve.tensor_tensor(comb[:, :, :], hot1, over(w1, NE), ALU.mult)
            link(dve.tensor_tensor(part, hot2, over(w2, NE), ALU.mult))
            link(dve.tensor_tensor(comb[:, :, :], comb[:, :, :], part, ALU.add))

            dve.wait_ge(rounds_done, 1)
            with dve.Fori(0, NQ) as q:
                first = dve.value_load(bounds[0:1, bass.ds(q, 1)], min_val=0, max_val=MAX_ROUNDS)
                end = dve.value_load(bounds[0:1, bass.ds(q + 1, 1)], min_val=1, max_val=MAX_ROUNDS)
                with dve.Fori(first, end) as c:
                    for t in range(TT):
                        mine = rank[:, t, bass.ds(q * QE, QE)]
                        dve.tensor_tensor(pick[:, t, :, :],
                                          slot_id[:, :].unsqueeze(1).to_broadcast([P, QE, SLOTS]),
                                          mine.unsqueeze(2).to_broadcast([P, QE, SLOTS]),
                                          ALU.is_equal).then_inc(round_link, 1)
                    dve.wait_ge(round_link, 4 * c + 2)
                    for t in range(TT):
                        dve.tensor_tensor(pickw[:, t, :, :], pick[:, t, :, :],
                                          comb[:, t, bass.ds(q * QE, QE)].unsqueeze(2).to_broadcast(
                                              [P, QE, SLOTS]), ALU.mult).then_inc(pick_done, 1)
                    dve.tensor_scalar(rank[:, :, bass.ds(q * QE, QE)], rank[:, :, bass.ds(q * QE, QE)],
                                      float(-SLOTS), None, ALU.add).then_inc(round_link, 1)
                    dve.wait_ge(xg_ps, 2 * c + 2)
                    dve.tensor_copy(xg[:, KC // 2:KC, :],
                                    bank[5][:, :].rearrange("p (k s) -> p k s", s=P)).then_inc(xg_v, 1)
                    dve.wait_ge(sg_done, c + 1)
                    dve.tensor_tensor(hs[:, :], sg[:, :], bank[6][:, 0:DE],
                                      ALU.mult).then_inc(round_link, 1)
                    dve.wait_ge(round_link, 4 * c + 4)
                    dve.tensor_tensor(hs[:, :], hs[:, :], bank[6][:, DE:2 * DE],
                                      ALU.mult).then_inc(bank_free[6], 1)
                    dve.wait_ge(y_ps, 2 * c + 2)
                    dve.tensor_copy(ys[:, HALF:DM], bank[5][:, :]).then_inc(bank_free[5], 1)
            total = dve.value_load(bounds[0:1, NQ:NQ + 1], min_val=NQ, max_val=MAX_ROUNDS)
            dve.wait_ge(added, 4 * total + 2)
            for t in range(TT):
                dve.bn_stats(stats[:, t, 0, :], bank[2 * t][:, :])
            for t in range(TT):
                dve.wait_ge(added, 4 * total + 3 + t)
                link(dve.bn_stats(stats[:, t, 1, :], bank[2 * t + 1][:, :]))
                variance(t)
            dve.wait_ge(ln_in, 64)
            for t in range(TT):
                for h in range(2):
                    cols = slice(h * HALF, (h + 1) * HALF)
                    ins = dve.scalar_tensor_tensor(x1[:, t, cols], bank[2 * t + h][:, :], moments[:, t, 0:1],
                                                   lng[:, cols], ALU.subtract, ALU.mult)
                link(ins)
                dve.wait_ge(rstd_done, TT + t + 1)
                for h in range(2):
                    cols = slice(h * HALF, (h + 1) * HALF)
                    dve.scalar_tensor_tensor(x1[:, t, cols], x1[:, t, cols], rstd[:, t:t + 1],
                                             lnb[:, cols], ALU.mult, ALU.add).then_inc(x1_done, 1)

        @block.tensor
        def _(pe):
            def low_words(n):
                s = n % NSPL
                return (wh[:, s, :].rearrange("p (k c) -> p k c", k=KC),
                        wl[:, s, :].rearrange("p (k c) -> p k c", k=KC))

            def product(dst, n, ks, high_in, low_in):
                h, l = low_words(n)
                for i, k in enumerate(ks):
                    for w, v in ((h, high_in), (h, low_in), (l, high_in)):
                        mm = pe.matmul(dst, w[:, k, :], v[:, i, :], start=(i == 0 and w is h and v is high_in),
                                       stop=(i == len(ks) - 1 and w is l))
                return mm

            def seed(signal):
                for t in range(TT):
                    for h in range(2):
                        mm = pe.matmul(bank[2 * t + h][:, :], alpha_i[:, :], x1[:, t, h * HALF:(h + 1) * HALF],
                                       start=True, stop=True, skip_group_check=True)
                        if signal:
                            mm.then_inc(added, 1)

            def attention(i):
                c = i // 3
                if i % 3 == 0 and 1 <= c <= CC:
                    d = c - 1
                    if d >= 1:
                        pe.wait_ge(pT_done, 2 * d)
                    for j in range(2):
                        pe.wait_ge(prob_done, 2 * d + j + 1)
                        for b in range(3):
                            mm = pe.transpose(bank[2 + j][:, b * P:(b + 1) * P], sc[:, j, b, :], ident[:, :])
                        mm.then_inc(pT_ps, 1)
                if i % 3 == 0 and c < CC:
                    if c >= 1:
                        pe.wait_ge(score_sb, 2 * c)
                    for j in range(2):
                        hp = slice(HD * j, HD * (j + 1))
                        pe.matmul(bank[j][:, 0:P], qT[hp, c, 0:P], kT[hp, c, 0:P], start=True, stop=True)
                    for j in range(2):
                        hp = slice(HD * j, HD * (j + 1))
                        pe.matmul(bank[j][:, P:3 * P], qT[hp, c, P:SEQ], kT[hp, c, :],
                                  start=True, stop=True).then_inc(score_ps, 1)
                if i % 3 == 2 and 1 <= c <= CC:
                    d = c - 1
                    pe.wait_ge(pT_done, 2 * d + 2)
                    if d >= 2:
                        pe.wait_ge(ol_done, d - 1)
                    if d == 0:
                        pe.wait_ge(bias_read, 1)
                    for b, keys in ((0, slice(0, 2)), (1, slice(2, 3))):
                        for j in range(2):
                            dst = bank[6 + d % 2][HD * j:HD * (j + 1), b * P:SEQ]
                            cols = slice((2 * d + j) * HD, (2 * d + j + 1) * HD)
                            mm = pe.matmul(dst, vv[:, b, cols],
                                           pT[:, j, keys, :].rearrange("p b q -> p (b q)"),
                                           start=(b == 0), stop=(b == 1), skip_group_check=True)
                    mm.then_inc(pv_ps, 1)

            pe.wait_ge(ident_done, 1)
            pe.wait_ge(x_in, 16 * TT)
            for b in range(KC // 2):
                for k in (2 * b, 2 * b + 1):
                    for t in range(TT):
                        mm = pe.transpose(bank[b][:, (k % 2) * SEQ + t * P:(k % 2) * SEQ + (t + 1) * P],
                                          x1[:, t, k::KC], ident[:, :])
                mm.then_inc(xT_ps, 1)
            pe.wait_ge(xl_done, KC // 2)

            for n in range(U0):
                kind, c = unit(n)
                if n >= UA:
                    if n == UA:
                        pe.wait_ge(evac_a, UA)
                    attention(n - UA)
                if n == 2:
                    pe.wait_ge(wrb_done, 1)
                    for k in range(KC):
                        mm = pe.matmul(bank[6][:, 0:NL], ones[:, :], wrb[:, k, :],
                                       start=(k == 0), stop=(k == KC - 1))
                    mm.then_inc(bias_ps, 1)
                if n == U0 - 1:
                    pe.wait_ge(consts, N_CONSTS)
                    pe.wait_ge(score_sb, NH)
                    pe.wait_ge(pT_done, NH)
                    seed(False)
                pe.wait_ge(lo_done, n + 1)
                if n < 2 * NA:
                    if n >= 2:
                        on_act, count = evacuated(n - 2)
                        pe.wait_ge(evac_a if on_act else evac_v, count)
                    dst = bank[4 + n % 2][:, 0:SEQ]
                else:
                    on_act, count = evacuated(2 * NA - 1 - (n == 2 * NA))
                    if c < 2 and kind == "ga":
                        pe.wait_ge(evac_a if on_act else evac_v, count)
                    half = 0 if kind == "ga" else 1
                    dst = bank[4 + n % 2][:, half * SEQ:(half + 1) * SEQ]
                if kind == "v":
                    t, s = n % 2, n // 2 * 2 % NSPL
                    if t == 0:
                        pe.wait_ge(lo_done, n + 2)
                    for k in range(KC):
                        ws = slice(k * P, (k + 1) * P)
                        for v, w in ((xh, wh), (xh, wl), (xl, wh)):
                            mm = pe.matmul(dst, v[:, k, t * P:(t + 1) * P], w[:, s:s + 2, ws],
                                           start=(k == 0 and v is xh and w is wh),
                                           stop=(k == KC - 1 and v is xl))
                else:
                    mm = product(dst, n, range(KC), xh, xl)
                mm.then_inc(unit_done, 1)

            def branches(j, m):
                pe.wait_ge(lo_done, UPJ * j + U0 + m + 1)
                product(bank[6 + m][:, 0:SEQ], U0 + m, range(CC), zh, zl)
                product(bank[6 + m][:, SEQ:2 * SEQ], U0 + m, range(CC, KC), oh, ol).then_inc(unit_done, 1)

            def merge(j, m, at, in_loop=True):
                n = U0 + at + m
                pe.wait_ge(lo_done, UPJ * j + n + 1)
                pe.wait_ge(yl_done, 2 * j + m + 1)
                s = n % NSPL
                for t in range(TT):
                    for v, w in ((yh, wh), (yh, wl), (yl, wh)):
                        for h in range(2):
                            mm = pe.matmul(bank[2 * t + h][:, :], v[:, m, t * P:(t + 1) * P],
                                           w[:, s, h * HALF:(h + 1) * HALF],
                                           start=False, stop=True, skip_group_check=True)
                    if m == 1 and not in_loop:
                        mm.then_inc(acc_done, 1)
                if in_loop or m == 0:
                    mm.then_inc(unit_done, 1)

            pe.wait_ge(ol_done, CC)
            pe.wait_ge(zl_done, CC)
            with pe.Fori(0, JP - 1) as j:
                for m in range(2):
                    branches(j, m)
                pe.wait_ge(sig_done, 2 * j + 2)
                for i in range(2, 6):
                    pe.wait_ge(lo_done, UPJ * j + U0 + i + 1)
                    half = i // 2 - 1
                    product(bank[4 + i % 2][:, half * SEQ:(half + 1) * SEQ], U0 + i, range(KC),
                            xh, xl).then_inc(unit_done, 1)
                for m in range(2):
                    merge(j, m, 6)
            for m in range(2):
                branches(JP - 1, m)
            for m in range(2):
                merge(JP - 1, m, 2, False)

            pe.wait_ge(y_done, KC)
            for t in range(TT):
                pe.wait_ge(norm_done, 2 * (t + 1))
                for k in range(KC):
                    mm = pe.transpose(bank[4 + 2 * t + k // 4][:, (k % 4) * P:(k % 4 + 1) * P],
                                      x1[:, t, k::KC], ident[:, :])
                    if k % 4 == 3:
                        mm.then_inc(x1T_ps, 1)
            for t in range(TT):
                pe.wait_ge(bank_free[4 + 2 * t], 1)
                pe.wait_ge(bank_free[5 + 2 * t], 1)
                for k in range(KC):
                    mm = pe.matmul(bank[4][:, t * NL:(t + 1) * NL], x1T[:, k, t * P:(t + 1) * P],
                                   wr[:, k, :], start=(k == 0), stop=(k == KC - 1))
            mm.then_inc(logit_ps, 1)
            pe.wait_ge(x1_done, TT)
            seed(True)
            pe.wait_ge(routed, 1)
            first, second = chosen[:, 0, :], chosen[:, 1, :]
            pe.matmul(bank[5][:, 0:NE], before[:, :], first, start=True, stop=True)
            pe.matmul(bank[5][:, NE:2 * NE], ones_b[:, :], first, start=True, stop=False)
            pe.matmul(bank[5][:, NE:2 * NE], before[:, :], second, start=False, stop=True)
            pe.matmul(bank[5][:, TT * NE:(TT + 1) * NE], ones_b[:, :], first, start=True, stop=False)
            pe.matmul(bank[5][:, TT * NE:(TT + 1) * NE], ones_b[:, :], second,
                      start=False, stop=True).then_inc(rank_ps, 1)

            pe.wait_ge(rounds_done, 1)
            with pe.Fori(0, NQ // 2) as o:
                for half in range(2):
                    q = 2 * o + half
                    w = gu[half]
                    first = pe.value_load(bounds[0:1, bass.ds(q, 1)], min_val=0, max_val=MAX_ROUNDS)
                    end = pe.value_load(bounds[0:1, bass.ds(q + 1, 1)], min_val=1, max_val=MAX_ROUNDS)
                    with pe.Fori(first, end) as c:
                        pe.wait_ge(pick_done, 2 * c + 2)
                        pe.wait_ge(bank_free[4], c + 1)
                        pe.wait_ge(bank_free[5], c + 1)
                        for k in range(KC):
                            for t in range(TT):
                                mm = pe.matmul(bank[4 + k // 4][:, (k % 4) * P:(k % 4 + 1) * P],
                                               x1[:, t, k::KC],
                                               pick[:, t, :, :].rearrange("p e s -> p (e s)"),
                                               start=(t == 0), stop=(t == TT - 1))
                            if k % 4 == 3:
                                mm.then_inc(xg_ps, 1)
                        pe.wait_ge(bank_free[7], c + 1)
                        for t in range(TT):
                            mm = pe.transpose(bank[7][:, SEQ + t * P:SEQ + (t + 1) * P],
                                              pickw[:, t, :, :].rearrange("p e s -> p (e s)"), ident[:, :])
                        mm.then_inc(put_ps, 1)
                        pe.wait_ge(xg_a, c + 1)
                        pe.wait_ge(xg_v, c + 1)
                        pe.wait_ge(bank_free[6], c + 1)
                        pe.wait_ge(gu_in[half], 2 * QE * 16 * (o + 2 - half))
                        for k in range(KC):
                            for e in range(QE):
                                g = slice(SLOTS * e, SLOTS * (e + 1))
                                mm = pe.matmul(bank[6][g, :], xg[:, k, g], w[:, e, k, :],
                                               start=(k == 0), stop=(k == KC - 1))
                        mm.then_inc(gu_ps, 1)
                        pe.wait_ge(bank_free[6], c + 2)
                        pe.wait_ge(put_done, c + 1)
                        for j in range(FC):
                            mm = pe.transpose(bank[7][:, j * P:(j + 1) * P], hs[:, j * P:(j + 1) * P],
                                              ident[:, :])
                        mm.then_inc(hT_ps, 1)
                        pe.wait_ge(bank_free[7], c + 2)
                        for h in range(2):
                            pe.wait_ge(dn_in[h], QE * 16 * (q + 1))
                            for j in range(FC):
                                for e in range(QE):
                                    g = slice(SLOTS * e, SLOTS * (e + 1))
                                    mm = pe.matmul(bank[4 + h][g, :], hT[:, j, g],
                                                   dn[:, e, j, h * HALF:(h + 1) * HALF],
                                                   start=(j == 0), stop=(j == FC - 1))
                            mm.then_inc(y_ps, 1)
                        for h in range(2):
                            pe.wait_ge(bank_free[4 + h], c + 2)
                            for t in range(TT):
                                pe.matmul(bank[2 * t + h][:, :], put[:, t * P:(t + 1) * P],
                                          ys[:, h * HALF:(h + 1) * HALF], start=False, stop=True,
                                          skip_group_check=True).then_inc(added, 1)


_INS = ['x', 'w_in', 'conv_w', 'w_out_conv', 'w_out_attn', 'w_o', 'ln1_g', 'ln1_b',
        'w_router_group', 'w_router_expert', 'w_gate', 'w_up', 'w_down', 'ln2_g', 'ln2_b']


def kernel(**inputs):
    import numpy as _np
    import concourse.bacc as _bacc
    from concourse import mybir as _mybir
    from concourse.bass_utils import run_bass_kernel_spmd as _run

    nc = _bacc.Bacc("TRN2", target_bir_lowering=False, num_devices=1)
    arrays, args = {}, []
    for name in _INS:
        a = _np.ascontiguousarray(inputs[name])
        arrays[f"in_{name}"] = a
        args.append(nc.dram_tensor(f"in_{name}", a.shape, _mybir.dt.from_np(a.dtype),
                                   kind="ExternalInput").ap())
    args.append(nc.dram_tensor("out_0", (1, SEQ, DM), _mybir.dt.float32, kind="ExternalOutput").ap())
    hybrid_block(nc, *args)
    r = _run(nc, [arrays], core_ids=[0])
    return r.results[0]["out_0"]
```

```python
import numpy as np
import concourse.bass as bass
from concourse import mybir
from contextlib import ExitStack

F32 = mybir.dt.float32
F32R = mybir.dt.float32r
BF16 = mybir.dt.bfloat16
I32 = mybir.dt.int32
ALU = mybir.AluOpType
ACT = mybir.ActivationFunctionType
AX = mybir.AxisListType

P = 128
SEQ, DM = 256, 1024
TT = SEQ // P
KC = DM // P
CW, AW = 512, 512
CC = CW // P
NH, HD = 8, 64
NG, EPG, DE = 4, 8, 256
NE = NG * EPG
FC = DE // P
QE = 4
NQ = NE // QE
SLOTS = P // QE
NL = NG + NE
EPS = 1e-5
ALPHA = 2.0 ** 0.25
SCALE = HD ** -0.5
MASKED = -1e30
MAX_ROUNDS = NQ + TT * SEQ // SLOTS
N_CONSTS = 11
N_SMALL = 16 * 7
FAR = 1e6
COL_B, COL_C, COL_X, COL_Q, COL_K, COL_V = (CW * i for i in range(6))
COL_GA = 3 * CW + 3 * AW
COL_GB = COL_GA + DM
GRP = 2 * P
NRAW, NSPL = 2, 4
HALF = 512
K_FIRST = 2
X1_PARTS = 3
WARM_X, WARM_UNIT, WARM_NORM = 8, 8, 4
WARM_ROUND = 4, 3


def hybrid_block(nc, x, w_in, conv_w, w_out_conv, w_out_attn, w_o, ln1_g, ln1_b,
                 w_router_group, w_router_expert, w_gate, w_up, w_down, ln2_g, ln2_b, out):
    x_v = x[0, :, :].rearrange("(t p) d -> p t d", p=P)
    out_v = out[0, :, :].rearrange("(t p) d -> p t d", p=P)
    win_v = w_in[0, :, :].rearrange("(p k) c -> p k c", k=KC)
    wc_v = w_out_conv[0, :, :].rearrange("(j p) d -> p j d", p=P)
    wa_v = w_out_attn[0, :, :].rearrange("(j p) d -> p j d", p=P)
    wo_v = w_o[0, :, :].rearrange("(j p) d -> p j d", p=P)
    convw_v = conv_w[0, :, :].rearrange("i (j p) -> p j i", p=P)
    gcol_v = ln1_g[0, :].rearrange("(p k) -> p k", k=KC)
    bcol_v = ln1_b[0, :].rearrange("(p k) -> p k", k=KC)
    wrg_v = w_router_group[0, :, :].rearrange("(p k) g -> p k g", k=KC)
    wre_v = w_router_expert[0, :, :].rearrange("(p k) e -> p k e", k=KC)
    wg_v = w_gate[0, :, :, :].rearrange("e (p k) f -> p e k f", k=KC)
    wu_v = w_up[0, :, :, :].rearrange("e (p k) f -> p e k f", k=KC)
    wd_v = w_down[0, :, :, :].rearrange("e (j p) d -> p e j d", p=P)

    ctx = ExitStack()
    with ctx:
        def sb(name, shape, dt=F32, where=ctx):
            return where.enter_context(nc.sbuf_tensor(name, shape, dt))

        def sem(name):
            return ctx.enter_context(nc.semaphore(name))

        x1 = sb("x1", [P, TT, DM])
        wr = sb("wr", [P, KC, NL])
        convw = sb("convw", [P, CC, 3])
        ident = sb("ident", [P, P])
        alpha_i = sb("alpha_i", [P, P])
        before = sb("before", [P, P], BF16)
        ones_b = sb("ones_b", [P, P], BF16)
        ones = sb("ones", [P, P])
        gcol = sb("gcol", [P, KC])
        bcol = sb("bcol", [P, KC])
        wrb = sb("wrb", [P, KC, NL])
        rbias = sb("rbias", [P, NL])
        chosen = sb("chosen", [P, TT, NE], BF16)
        slot_id = sb("slot_id", [P, SLOTS])
        group_key = sb("group_key", [P, NG])
        expert_key = sb("expert_key", [P, NE])
        half_neg = sb("half_neg", [P, TT])
        stats = sb("stats", [P, TT, 2, 6])
        moments = sb("moments", [P, TT, 2])
        rstd = sb("rstd", [P, TT])
        shift = sb("shift", [P, 1])
        rt = sb("rt", [P, 13, TT, NL])
        rs = sb("rs", [P, 16, TT])
        rounds_f = sb("rounds_f", [P, 4, 16])
        rounds_i = sb("rounds_i", [P, 1, 16], I32)
        bounds = sb("bounds", [P, 16], I32)
        quad_of = sb("quad_of", [P, MAX_ROUNDS + 1], I32)
        round_id = sb("round_id", [P, MAX_ROUNDS + 1])
        passed = sb("passed", [P, MAX_ROUNDS + 1, NQ])
        quad_f = sb("quad_f", [P, MAX_ROUNDS + 1])
        rank = sb("rank", [P, TT, NE])
        comb = sb("comb", [P, TT, NE])

        gu0 = sb("gu0", [P, QE, KC, 2 * DE])
        dn_scope = ExitStack()
        qT = sb("qT", [P, CC, SEQ], where=dn_scope)
        kT = sb("kT", [P, CC, SEQ], where=dn_scope)
        vv = sb("vv", [P, TT, AW], where=dn_scope)
        dist = sb("dist", [P, 3, P], where=dn_scope)
        sc = sb("sc", [P, 2, 3, P], where=dn_scope)
        pT = sb("pT", [P, 2, 3, P], where=dn_scope)
        nmax = sb("nmax", [P, 2, 2], where=dn_scope)
        rsum = sb("rsum", [P, 2, 2], where=dn_scope)
        rinv = sb("rinv", [P, 2, 2], where=dn_scope)
        cc_t = sb("cc_t", [P, 2, SEQ], where=dn_scope)
        u_t = sb("u_t", [P, 2, 2 + SEQ], where=dn_scope)
        cv_t = sb("cv_t", [P, 2, SEQ], where=dn_scope)
        z_t = sb("z_t", [P, SEQ], where=dn_scope)
        dn_scope.close()
        dn = sb("dn", [P, QE, FC, DM])

        mix_scope = ExitStack()
        xh = sb("xh", [P, KC, SEQ], F32R, mix_scope)
        xl = sb("xl", [P, KC, SEQ], F32R, mix_scope)
        raw = sb("raw", [P, NRAW, KC * GRP], where=mix_scope)
        wh = sb("wh", [P, NSPL, KC * P], F32R, mix_scope)
        wl = sb("wl", [P, NSPL, KC * P], F32R, mix_scope)
        zh = sb("zh", [P, CC, SEQ], F32R, mix_scope)
        zl = sb("zl", [P, CC, SEQ], F32R, mix_scope)
        oh = sb("oh", [P, CC, SEQ], F32R, mix_scope)
        ol = sb("ol", [P, CC, SEQ], F32R, mix_scope)
        yh = sb("yh", [P, 2, SEQ], F32R, mix_scope)
        yl = sb("yl", [P, 2, SEQ], F32R, mix_scope)
        sig = sb("sig", [P, 2, 2 * SEQ], where=mix_scope)
        yt = sb("yt", [P, 2, SEQ], where=mix_scope)
        mix_scope.close()
        gu1 = sb("gu1", [P, QE, KC, 2 * DE])
        lng = sb("lng", [P, DM])
        lnb = sb("lnb", [P, DM])
        x1T_scope = ExitStack()
        x1T = sb("x1T", [P, KC, SEQ], where=x1T_scope)
        x1T_scope.close()
        xg = sb("xg", [P, KC, P])
        ys = sb("ys", [P, DM])
        pick = sb("pick", [P, TT, QE, SLOTS])
        pickw = sb("pickw", [P, TT, QE, SLOTS])
        put = sb("put", [P, SEQ])
        sg = sb("sg", [P, DE])
        hs = sb("hs", [P, DE])
        hT = sb("hT", [P, FC, P])

        bank = [ctx.enter_context(nc.psum_tensor(f"bank{i}", [P, HALF], F32)) for i in range(8)]

        gu = [gu0, gu1]
        result = gu0[:, 0, :, :].rearrange("p k c -> p (k c)")[:, 0:TT * DM].rearrange(
            "p (t d) -> p t d", t=TT)
        e_in, e_out = (rt[:, i, :, 0:NG + 1] for i in (11, 12))

        x_in = sem("x_in")
        small_in = sem("small_in")
        raw_in = [sem(f"raw_in{i}") for i in range(NRAW)]
        ln_in = sem("ln_in")
        gu_in = [[sem(f"gu_in{i}_{k}") for k in range(2)] for i in range(2)]
        dn_in = [sem(f"dn_in{i}") for i in range(2)]
        out_done = sem("out_done")
        ident_done = sem("ident_done")
        consts = sem("consts")
        pool_link = sem("pool_link")
        xT_ps = sem("xT_ps")
        xh_done = sem("xh_done")
        xl_done = sem("xl_done")
        hi_done = sem("hi_done")
        lo_done = sem("lo_done")
        unit_done = sem("unit_done")
        evac_a = sem("evac_a")
        evac_v = sem("evac_v")
        score_ps = sem("score_ps")
        score_sb = sem("score_sb")
        exp_done = sem("exp_done")
        prob_done = sem("prob_done")
        pT_ps = sem("pT_ps")
        pT_done = sem("pT_done")
        pv_ps = sem("pv_ps")
        oh_done = sem("oh_done")
        ol_done = sem("ol_done")
        z_done = sem("z_done")
        zh_done = sem("zh_done")
        zl_done = sem("zl_done")
        sig_done = sem("sig_done")
        y_done = sem("y_done")
        yh_done = sem("yh_done")
        yl_done = sem("yl_done")
        dve_link = sem("dve_link")
        nmax_done = sem("nmax_done")
        moment_done = sem("moment_done")
        rstd_done = sem("rstd_done")
        shift_done = sem("shift_done")
        norm_done = [sem(f"norm_done{t}") for t in range(TT)]
        acc_done = sem("acc_done")
        wrb_done = sem("wrb_done")
        bias_ps = sem("bias_ps")
        bias_read = sem("bias_read")
        x1_done = sem("x1_done")
        x1T_ps = sem("x1T_ps")
        logit_ps = sem("logit_ps")
        gexp_in = sem("gexp_in")
        gexp_done = sem("gexp_done")
        routed = sem("routed")
        rank_ps = sem("rank_ps")
        rank_read = sem("rank_read")
        rounds_done = sem("rounds_done")
        y_link = sem("y_link")
        last_normed = sem("last_normed")
        last_done = sem("last_done")
        round_link = sem("round_link")
        bank_free = {b: sem(f"bank_free{b}") for b in (4, 5, 6, 7)}
        pick_done = sem("pick_done")
        xg_ps = sem("xg_ps")
        xg_a = sem("xg_a")
        xg_v = sem("xg_v")
        put_ps = sem("put_ps")
        put_done = sem("put_done")
        gu_part = sem("gu_part")
        gu_ps = sem("gu_ps")
        pickw_done = sem("pickw_done")
        sg_done = sem("sg_done")
        hT_ps = sem("hT_ps")
        y_ps = sem("y_ps")
        added = sem("added")

        phase_a = ([("q", 0), ("q", 1), ("k", 0), ("k", 1), ("v", 0), ("v", 1)]
                   + [(n, c) for c in range(CC // 2) for n in ("cc", "cx", "cb")])
        lead = [("ga", 0), ("gb", 0)]
        NA = len(phase_a)
        PB = NA + len(lead)
        JP = KC // 2
        START = {"q": COL_Q, "k": COL_K, "v": COL_V, "cc": COL_C, "cx": COL_X, "cb": COL_B,
                 "ga": COL_GA, "gb": COL_GB}

        sequence = (phase_a + lead
                    + [x for j in range(JP - 1) for x in (("ca", j), ("ga", j + 1), ("gb", j + 1), ("wo", j))]
                    + [("ca", JP - 1), ("wo", JP - 1)])
        UNITS = 2 * len(sequence)
        U0 = 2 * PB
        UPJ = 8
        UA = 12
        assert U0 % NSPL == 0 and PB % NRAW == 0 and UPJ % NSPL == 0

        def unit(n):
            return sequence[n // 2][0], 2 * sequence[n // 2][1] + n % 2

        def evacuated(n):
            mine = ("q", "k", "v", "cc")
            on_act = unit(n)[0] in mine
            return on_act, sum((unit(m)[0] in mine) == on_act for m in range(n + 1))

        block = ctx.enter_context(nc.Block())

        @block.sync
        def _(sp):
            def load_pair(slot, kind, idx):
                s = raw_in[slot]
                dst = raw[:, slot, :].rearrange("p (k c) -> p k c", k=KC)
                if kind in START:
                    for k in (0, KC // 2):
                        sp.dma_start(dst[:, k:k + KC // 2, :],
                                     win_v[:, k:k + KC // 2, bass.ds(idx * GRP + START[kind], GRP)]
                                     ).then_inc(s, 16)
                elif kind == "ca":
                    sp.dma_start(dst[:, 0:CC, :], wc_v[:, :, bass.ds(idx * GRP, GRP)]).then_inc(s, 16)
                    sp.dma_start(dst[:, CC:KC, :], wa_v[:, :, bass.ds(idx * GRP, GRP)]).then_inc(s, 16)
                else:
                    for i in range(2):
                        sp.dma_start(dst[:, :, i * P:(i + 1) * P],
                                     wo_v[:, bass.ds(idx * 2 + i, 1), :].rearrange(
                                         "p a (k c) -> p (a k) c", k=KC)).then_inc(s, 16)

            def load_gu(h, q, part, experts=range(QE)):
                ks = slice(0, K_FIRST) if part == 0 else slice(K_FIRST, KC)
                for e in experts:
                    for c, src in ((0, wg_v), (DE, wu_v)):
                        sp.dma_start(gu[h][:, e, ks, c:c + DE],
                                     src[:, bass.ds(q * QE + e, 1), ks, :]).then_inc(gu_in[h][part], 16)

            def load_dn_half(h, q, e):
                sp.dma_start(dn[:, bass.ds(e, 1), :, h * HALF:(h + 1) * HALF],
                             wd_v[:, bass.ds(q * QE + e, 1), :, h * HALF:(h + 1) * HALF]
                             ).then_inc(dn_in[h], 16)

            def load_dn(q):
                for h in range(2):
                    for e in range(QE):
                        load_dn_half(h, q, e)

            for t in range(TT):
                sp.dma_start(x1[:, t, :], x_v[:, t, :]).then_inc(x_in, 16)
            ahead = [(e, c, k) for k in range(2) for e in range(QE) for c in range(2)]
            for n in range(PB):
                if n >= NRAW:
                    sp.wait_ge(lo_done, 2 * (n - NRAW + 1))
                load_pair(n % NRAW, *sequence[n])
                if n == 1:
                    for dst, src in ((wr[:, :, 0:NG], wrg_v), (wr[:, :, NG:NL], wre_v),
                                     (gcol[:, :], gcol_v), (bcol[:, :], bcol_v),
                                     (convw[:, :, 0], convw_v[:, :, 0]), (convw[:, :, 1], convw_v[:, :, 1]),
                                     (convw[:, :, 2], convw_v[:, :, 2])):
                        sp.dma_start(dst, src, allow_slow_non_contiguous=True).then_inc(small_in, 16)
                for _ in range(0 if n < NRAW else 2 if n % 3 == 0 else 1):
                    if ahead:
                        e, c, k = ahead.pop(0)
                        ks = slice(0, K_FIRST) if k == 0 else slice(K_FIRST, KC)
                        sp.dma_start(gu0[:, e, ks, c * DE:(c + 1) * DE],
                                     (wg_v, wu_v)[c][:, e, ks, :]).then_inc(gu_in[0][k], 16)
            assert not ahead
            with sp.Fori(0, JP - 1) as j:
                for i, (kind, idx) in enumerate((("ca", j), ("ga", j + 1), ("gb", j + 1), ("wo", j))):
                    sp.wait_ge(lo_done, UPJ * j + 2 * (PB + i - NRAW + 1))
                    load_pair((PB + i) % NRAW, kind, idx)
                    if i % 2 == 1:
                        sp.wait_ge(pv_ps, CC)
                        sp.wait_ge(zl_done, CC)
                        load_dn_half(i // 2, 0, j)
            for n in range(len(sequence) - 2, len(sequence)):
                sp.wait_ge(lo_done, 2 * (n - NRAW + 1))
                load_pair(n % NRAW, *sequence[n])
            for h in range(2):
                load_dn_half(h, 0, QE - 1)
            for e, ready, count in ((0, unit_done, UNITS - 6),
                                    (1, lo_done, UNITS),
                                    (2, acc_done, TT), (3, acc_done, TT)):
                sp.wait_ge(ready, count)
                for part in range(2):
                    load_gu(1, 1, part, [e])

            sp.wait_ge(rounds_done, 1)

            def through(q):
                return sp.value_load(bounds[0:1, bass.ds(q, 1)], min_val=1, max_val=MAX_ROUNDS)

            def load_quad(h, q, last=False):
                rounds = through(q - 1)
                sp.wait_ge(gu_part, rounds)
                load_gu(h, q, 0)
                if last:
                    sp.wait_ge(y_ps, 2 * rounds)
                    load_dn(q - 1)
                    load_gu(h, q, 1)
                else:
                    sp.wait_ge(gu_ps, rounds)
                    load_gu(h, q, 1)
                    sp.wait_ge(y_ps, 2 * rounds)
                    load_dn(q - 1)

            with sp.Fori(1, NQ // 2 - 1) as o:
                for h in range(2):
                    load_quad(h, 2 * o + h)
            load_quad(0, NQ - 2)
            load_quad(1, NQ - 1, last=True)
            sp.wait_ge(y_ps, 2 * through(NQ - 1))
            load_dn(NQ - 1)
            for t in range(TT):
                for h in range(2):
                    cols = slice(h * HALF, (h + 1) * HALF)
                    if (t, h) == (TT - 1, 1):
                        sp.wait_ge(last_done, 1)
                    else:
                        sp.wait_ge(x1_done, X1_PARTS + 2 * t + h + 1)
                    sp.dma_start(out_v[:, t, cols], result[:, t, cols]).then_inc(out_done, 16)
            sp.wait_ge(out_done, 16 * 2 * TT)

        @block.gpsimd
        def _(pool):
            linked = [0]

            def link(ins):
                linked[0] += 1
                ins.then_inc(pool_link, 1)
                pool.wait_ge(pool_link, linked[0])

            def const(ins):
                ins.then_inc(consts, 1)

            link(pool.memset(ident[:, :], 0.0))
            pool.affine_select(out=ident[:, :], in_=ident[:, :], compare_op=ALU.not_equal, fill=1.0,
                               base=0, pattern=[[-1, P]], channel_multiplier=1).then_inc(ident_done, 1)
            link(pool.iota(dist[:, 0, :], pattern=[[1, P]], base=0, channel_multiplier=-1,
                           allow_small_or_imprecise_dtypes=True))
            link(pool.affine_select(out=dist[:, 0, :], in_=dist[:, 0, :], compare_op=ALU.is_ge,
                                    fill=MASKED, base=0, pattern=[[-1, P]], channel_multiplier=1))
            const(pool.iota(dist[:, 1, :], pattern=[[1, P]], base=-P, channel_multiplier=-1,
                            allow_small_or_imprecise_dtypes=True))
            const(pool.tensor_copy(dist[:, 2, :], dist[:, 0, :]))
            link(pool.memset(alpha_i[:, :], 0.0))
            const(pool.affine_select(out=alpha_i[:, :], in_=alpha_i[:, :], compare_op=ALU.not_equal,
                                     fill=ALPHA, base=0, pattern=[[-1, P]], channel_multiplier=1))
            link(pool.memset(before[:, :], 1.0))
            const(pool.affine_select(out=before[:, :], in_=before[:, :], compare_op=ALU.is_gt, fill=0.0,
                                     base=0, pattern=[[1, P]], channel_multiplier=-1))
            const(pool.memset(ones[:, :], 1.0))
            const(pool.memset(ones_b[:, :], 1.0))
            const(pool.iota(slot_id[:, :], pattern=[[1, SLOTS]], base=0, channel_multiplier=0,
                            allow_small_or_imprecise_dtypes=True))
            const(pool.iota(group_key[:, :], pattern=[[-1, NG]], base=NG, channel_multiplier=0,
                            allow_small_or_imprecise_dtypes=True))
            const(pool.iota(expert_key[:, :], pattern=[[-1, NE]], base=NE, channel_multiplier=0,
                            allow_small_or_imprecise_dtypes=True))
            const(pool.iota(round_id[:, :], pattern=[[1, MAX_ROUNDS + 1]], base=0, channel_multiplier=0,
                            allow_small_or_imprecise_dtypes=True))
            const(pool.memset(half_neg[:, :], -0.5))
            pool.wait_ge(consts, N_CONSTS)
            for n, (g, b) in enumerate(((ln1_g, ln1_b), (ln2_g, ln2_b))):
                if n == 0:
                    pool.wait_ge(unit_done, UNITS - 2)
                else:
                    pool.wait_ge(x1_done, X1_PARTS)
                pool.dma_start(lng[:, :], g[0:1, :].broadcast_to([P, DM])).then_inc(ln_in, 16)
                pool.dma_start(lnb[:, :], b[0:1, :].broadcast_to([P, DM])).then_inc(ln_in, 16)
                for t in range(TT):
                    pool.wait_ge(moment_done, TT * n + t + 1)
                    pool.tensor_tensor(rstd[:, t:t + 1], moments[:, t, 1:2], half_neg[:, 0:1],
                                       ALU.pow).then_inc(rstd_done, 1)
                    if t == n:
                        pool.wait_ge(rstd_done, TT * n + t + 1)
                        link(pool.tensor_tensor(shift[:, 0:1], moments[:, t, 0:1], rstd[:, t:t + 1], ALU.mult))
                        pool.tensor_scalar(shift[:, 0:1], shift[:, 0:1], -1.0, None,
                                           ALU.mult).then_inc(shift_done, 1)
                if n == 0:
                    cols = slice(HALF, DM)
                    pool.wait_ge(ln_in, 32)
                    pool.wait_ge(x1T_ps, 4)
                    link(pool.tensor_tensor(x1[:, 1, cols], x1[:, 1, cols], lng[:, cols], ALU.mult))
                    pool.tensor_tensor(x1[:, 1, cols], x1[:, 1, cols], lnb[:, cols],
                                       ALU.add).then_inc(x1_done, 1)
            pool.wait_ge(ln_in, 64)
            pool.wait_ge(last_normed, 1)
            link(pool.tensor_tensor(result[:, 1, cols], result[:, 1, cols], lng[:, cols], ALU.mult))
            pool.tensor_tensor(result[:, 1, cols], result[:, 1, cols], lnb[:, cols],
                               ALU.add).then_inc(last_done, 1)

        @block.scalar
        def _(act):
            def high(n, j=None):
                pair, s, more = n // 2, n % NSPL, 0 if j is None else j
                if n % 2 == 0:
                    act.wait_ge(raw_in[pair % NRAW], more * 16 * UPJ // NRAW + 32 * (pair // NRAW + 1))
                if n >= NSPL:
                    by_pair = n % 2 == 0 and unit(n - NSPL)[0] == "v"
                    act.wait_ge(unit_done, more * UPJ + n - NSPL + 1 + by_pair)
                act.activation(wh[:, s, :].rearrange("p (k c) -> p k c", k=KC),
                               raw[:, pair % NRAW, :].rearrange("p (k c) -> p k c", k=KC)
                               [:, :, n % 2 * P:(n % 2 + 1) * P], ACT.Copy).then_inc(hi_done, 1)

            def attention(i):
                c = i // 3
                if i % 3 == 0 and 1 <= c <= CC:
                    for j in range(2):
                        act.wait_ge(pT_ps, 2 * (c - 1) + j + 1)
                        if c >= 2:
                            act.wait_ge(pv_ps, c - 1)
                        act.activation(pT[:, j, :, :],
                                       bank[2 + j][:, 0:3 * P].rearrange("p (b q) -> p b q", b=3),
                                       ACT.Copy).then_inc(pT_done, 1)
                if i % 3 == 0 and c < CC:
                    for j in range(2):
                        act.wait_ge(nmax_done, 2 * c + j + 1)
                        act.activation(sc[:, j, 0, :], sc[:, j, 0, :], ACT.Exp, bias=nmax[:, j, 0:1],
                                       accum_out=rsum[:, j, 0:1])
                        act.activation(sc[:, j, 1:3, :], sc[:, j, 1:3, :], ACT.Exp,
                                       bias=nmax[:, j, 1:2], accum_out=rsum[:, j, 1:2]
                                       ).then_inc(exp_done, 1)
                if i % 3 == 2 and 1 <= c <= CC:
                    act.wait_ge(pv_ps, c)
                    act.activation(oh[:, c - 1, :], bank[6 + (c - 1) % 2][:, 0:SEQ],
                                   ACT.Copy).then_inc(oh_done, 1)

            for b in range(KC // 2):
                act.wait_ge(xT_ps, b + 1)
                act.activation(xh[:, 2 * b:2 * b + 2, :],
                               bank[b][:, :].rearrange("p (k s) -> p k s", k=2),
                               ACT.Copy).then_inc(xh_done, 1)
            for n in range(NSPL):
                high(n)

            for n in range(U0):
                kind, c = unit(n)
                src = bank[4 + n % 2][:, 0:SEQ]
                if n >= UA:
                    attention(n - UA)
                if kind in ("q", "k", "v", "cc"):
                    act.wait_ge(unit_done, n + 1)
                if kind == "q":
                    act.activation(qT[:, c, :], src, ACT.Copy, scale=SCALE).then_inc(evac_a, 1)
                elif kind == "k":
                    act.activation(kT[:, c, :], src, ACT.Copy).then_inc(evac_a, 1)
                elif kind == "v":
                    act.activation(vv[:, n % 2, c // 2 * GRP:(c // 2 + 1) * GRP], src,
                                   ACT.Copy).then_inc(evac_a, 1)
                elif kind == "cc":
                    if c >= 2:
                        act.wait_ge(evac_v, evacuated(n - 4)[1])
                    act.activation(cc_t[:, c % 2, :], src, ACT.Copy).then_inc(evac_a, 1)
                high(n + NSPL)
                if kind == "cb":
                    act.wait_ge(z_done, c + 1)
                    act.activation(zh[:, c, :], z_t[:, :], ACT.Copy).then_inc(zh_done, 1)

            def gates():
                for m in range(2):
                    act.activation(sig[:, m, :], bank[4 + m][:, :], ACT.Sigmoid).then_inc(sig_done, 1)

            def y_high(j, m):
                act.wait_ge(y_done, 2 * j + m + 1)
                act.activation(yh[:, m, :], yt[:, m, :], ACT.Copy).then_inc(yh_done, 1)

            act.wait_ge(unit_done, U0)
            gates()
            with act.Fori(0, JP - 1) as j:
                for i in range(UPJ):
                    high(U0 + i + NSPL, j)
                    if i in (1, 2):
                        y_high(j, i - 1)
                    if i == 5:
                        act.wait_ge(unit_done, UPJ * j + U0 + 6)
                        gates()
            for m in range(2):
                y_high(JP - 1, m)

            act.wait_ge(shift_done, 1)
            for h in range(2):
                act.activation(x1[:, 0, h * HALF:(h + 1) * HALF], bank[h][:, :], ACT.Identity,
                               scale=rstd[:, 0:1], bias=shift[:, 0:1]).then_inc(norm_done[0], 1)
            for t in range(TT):
                for g in range(2):
                    b = 4 + 2 * t + g
                    act.wait_ge(x1T_ps, b - 3)
                    act.activation(x1T[:, g * KC // 2:(g + 1) * KC // 2, t * P:(t + 1) * P],
                                   bank[b][:, :].rearrange("p (k s) -> p k s", s=P),
                                   ACT.Copy).then_inc(bank_free[b], 1)

            def take_gathered(n):
                act.wait_ge(xg_ps, 2 * n - 1)
                act.activation(xg[:, 0:KC // 2, :], bank[4][:, :].rearrange("p (k s) -> p k s", s=P),
                               ACT.Copy).then_inc(xg_a, 1)

            def compute(n):
                act.wait_ge(gu_ps, n)
                act.activation(sg[:, :], bank[6][:, 0:DE], ACT.Sigmoid).then_inc(sg_done, 1)
                act.wait_ge(put_ps, n)
                act.activation(put[:, :], bank[7][:, SEQ:2 * SEQ], ACT.Copy).then_inc(put_done, 1)
                act.wait_ge(hT_ps, n)
                act.activation(hT[:, :, :], bank[7][:, 0:SEQ].rearrange("p (j s) -> p j s", j=FC),
                               ACT.Copy).then_inc(bank_free[7], 1)
                act.wait_ge(y_ps, 2 * n - 1)
                act.activation(ys[:, 0:HALF], bank[4][:, :], ACT.Copy).then_inc(bank_free[4], 1)

            take_gathered(1)
            act.wait_ge(gexp_in, 1)
            act.activation(e_out, e_in, ACT.Exp).then_inc(gexp_done, 1)
            act.wait_ge(rounds_done, 1)
            last = act.value_load(bounds[0:1, NQ + 1:NQ + 2], min_val=NQ - 1, max_val=MAX_ROUNDS)
            with act.Fori(0, last) as c:
                compute(c + 1)
                take_gathered(c + 2)
            compute(last + 1)
            act.wait_ge(shift_done, 2)
            act.activation(result[:, 1, HALF:DM], bank[3][:, :], ACT.Identity, scale=rstd[:, 1:2],
                           bias=shift[:, 0:1]).then_inc(last_normed, 1)

        @block.vector
        def _(dve):
            linked = [0]

            def link(ins):
                linked[0] += 1
                ins.then_inc(dve_link, 1)
                dve.wait_ge(dve_link, linked[0])

            def low(n, j=None):
                pair, s, more = n // 2, n % NSPL, 0 if j is None else j
                dve.wait_ge(hi_done, more * UPJ + n + 1)
                dve.tensor_tensor(wl[:, s, :].rearrange("p (k c) -> p k c", k=KC),
                                  raw[:, pair % NRAW, :].rearrange("p (k c) -> p k c", k=KC)
                                  [:, :, n % 2 * P:(n % 2 + 1) * P],
                                  wh[:, s, :].bitcast(F32).rearrange("p (k c) -> p k c", k=KC),
                                  ALU.subtract).then_inc(lo_done, 1)

            def attention(i):
                c = i // 3
                if i % 3 == 0 and c < CC:
                    for j in range(2):
                        dve.wait_ge(score_ps, 2 * c + j + 1)
                        if c >= 1:
                            dve.wait_ge(pT_ps, 2 * c)
                        dve.scalar_tensor_tensor(
                            sc[:, j, :, :], dist[:, :, :], float(2.0 ** (-8.0 * (2 * c + j + 1) / NH)),
                            bank[j][:, 0:3 * P].rearrange("p (b k) -> p b k", b=3),
                            ALU.mult, ALU.add).then_inc(score_sb, 1)
                    for j in range(2):
                        dve.wait_ge(score_sb, 2 * c + j + 1)
                        dve.tensor_reduce(nmax[:, j, 0:1], sc[:, j, 0, :], AX.X, ALU.max, negate=True)
                        dve.tensor_reduce(nmax[:, j, 1:2], sc[:, j, 1:3, :], AX.XY, ALU.max,
                                          negate=True).then_inc(nmax_done, 1)
                if i % 3 == 1 and c < CC:
                    dve.wait_ge(exp_done, 2 * c + 2)
                    link(dve.reciprocal(rinv[:, :, :], rsum[:, :, :]))
                    for j in range(2):
                        dve.tensor_scalar(sc[:, j, 0, :], sc[:, j, 0, :], rinv[:, j, 0:1], None, ALU.mult)
                        dve.tensor_scalar(sc[:, j, 1:3, :], sc[:, j, 1:3, :], rinv[:, j, 1:2], None,
                                          ALU.mult).then_inc(prob_done, 1)
                if i % 3 == 2 and 1 <= c <= CC:
                    dve.wait_ge(oh_done, c)
                    dve.tensor_tensor(ol[:, c - 1, :], bank[6 + (c - 1) % 2][:, 0:SEQ],
                                      oh[:, c - 1, :].bitcast(F32), ALU.subtract).then_inc(ol_done, 1)

            dve.memset(rounds_f[:, :, :], 0.0)
            link(dve.memset(u_t[:, :, 0:2], 0.0))
            for b in range(KC // 2):
                dve.wait_ge(xh_done, b + 1)
                dve.tensor_tensor(xl[:, 2 * b:2 * b + 2, :],
                                  bank[b][:, :].rearrange("p (k s) -> p k s", k=2),
                                  xh[:, 2 * b:2 * b + 2, :].bitcast(F32),
                                  ALU.subtract).then_inc(xl_done, 1)
            for n in range(NSPL):
                low(n)
            dve.wait_ge(consts, N_CONSTS)
            dve.wait_ge(small_in, N_SMALL)
            gb, bb = (v[:, :].unsqueeze(2).to_broadcast([P, KC, NL]) for v in (gcol, bcol))
            link(dve.tensor_tensor(wrb[:, :, :], wr[:, :, :], bb, ALU.mult))
            dve.tensor_tensor(wr[:, :, :], wr[:, :, :], gb, ALU.mult).then_inc(wrb_done, 1)
            for n in range(U0):
                kind, c = unit(n)
                src = bank[4 + n % 2][:, 0:SEQ]
                u, cv = u_t[:, c % 2, :], cv_t[:, c % 2, :]
                if n >= UA:
                    attention(n - UA)
                if kind == "cx":
                    dve.wait_ge(unit_done, n + 1)
                    dve.wait_ge(evac_a, evacuated(n - 2)[1])
                    dve.tensor_tensor(u[:, 2:], src, cc_t[:, c % 2, :], ALU.mult).then_inc(evac_v, 1)
                if kind == "cb":
                    dve.wait_ge(unit_done, n + 1)
                    dve.tensor_tensor(z_t[:, :], src, cv, ALU.mult).then_inc(evac_v, 1)
                    dve.wait_ge(evac_v, evacuated(n)[1])
                    dve.engine_nop().then_inc(z_done, 1)
                low(n + NSPL)
                if kind == "cx":
                    dve.wait_ge(evac_v, evacuated(n)[1])
                    link(dve.tensor_scalar(cv, u[:, 2:], convw[:, c, 2:3], None, ALU.mult))
                    link(dve.scalar_tensor_tensor(cv, u[:, 1:1 + SEQ], convw[:, c, 1:2], cv,
                                                  ALU.mult, ALU.add))
                    link(dve.scalar_tensor_tensor(cv, u[:, 0:SEQ], convw[:, c, 0:1], cv,
                                                  ALU.mult, ALU.add))
                if kind == "cb":
                    dve.wait_ge(zh_done, c + 1)
                    dve.tensor_tensor(zl[:, c, :], z_t[:, :], zh[:, c, :].bitcast(F32),
                                      ALU.subtract).then_inc(zl_done, 1)
                    dve.wait_ge(zl_done, c + 1)

            def y_chunk(j, m):
                dve.wait_ge(unit_done, UPJ * j + U0 + m + 1)
                dve.wait_ge(sig_done, 2 * j + m + 1)
                dve.tensor_tensor(sig[:, m, :], sig[:, m, :], bank[6 + m][:, :],
                                  ALU.mult).then_inc(y_link, 1)
                dve.wait_ge(y_link, 2 * j + m + 1)
                dve.tensor_tensor(yt[:, m, :], sig[:, m, 0:SEQ], sig[:, m, SEQ:2 * SEQ],
                                  ALU.add).then_inc(y_done, 1)

            def y_low(j, m):
                dve.wait_ge(yh_done, 2 * j + m + 1)
                dve.tensor_tensor(yl[:, m, :], yt[:, m, :], yh[:, m, :].bitcast(F32),
                                  ALU.subtract).then_inc(yl_done, 1)

            with dve.Fori(0, JP - 1) as j:
                for i in range(UPJ):
                    if i < 2:
                        y_chunk(j, i)
                    low(U0 + i + NSPL, j)
                    if i in (2, 3):
                        y_low(j, i - 2)
            for m in range(2):
                y_chunk(JP - 1, m)
            for m in range(2):
                y_low(JP - 1, m)

            def variance(t):
                link(dve.bn_aggr(moments[:, t, :], stats[:, t, :, :]))
                dve.tensor_scalar(moments[:, t, 1:2], moments[:, t, 1:2], EPS, None,
                                  ALU.add).then_inc(moment_done, 1)

            for t in range(TT):
                dve.wait_ge(acc_done, t + 1)
                dve.bn_stats(stats[:, t, 0, :], bank[2 * t][:, :])
                link(dve.bn_stats(stats[:, t, 1, :], bank[2 * t + 1][:, :]))
                variance(t)
            dve.wait_ge(rstd_done, 2)
            for h in range(2):
                dve.tensor_scalar(x1[:, 1, h * HALF:(h + 1) * HALF], bank[2 + h][:, :], moments[:, 1, 0:1],
                                  rstd[:, 1:2], ALU.subtract, ALU.mult).then_inc(norm_done[1], 1)
            dve.wait_ge(bias_ps, 1)
            dve.tensor_copy(rbias[:, :], bank[6][:, 0:NL]).then_inc(bias_read, 1)
            dve.wait_ge(ln_in, 32)
            for t, cols in ((0, slice(0, DM)), (1, slice(0, HALF))):
                dve.wait_ge(x1T_ps, 2 * t + 2)
                link(dve.tensor_tensor(x1[:, t, cols], x1[:, t, cols], lng[:, cols], ALU.mult))
                dve.tensor_tensor(x1[:, t, cols], x1[:, t, cols], lnb[:, cols],
                                  ALU.add).then_inc(x1_done, 1)

            def over(v, n):
                return v.unsqueeze(2).to_broadcast([P, TT, n])

            def first_max(v, key, n, top, eq, hot, scratch):
                link(dve.tensor_reduce(top, v, AX.X, ALU.max))
                for t in range(TT):
                    ins = dve.scalar_tensor_tensor(eq[:, t, :], v[:, t, :], top[:, t:t + 1], key,
                                                   ALU.is_ge, ALU.mult)
                link(ins)
                link(dve.tensor_reduce(scratch, eq, AX.X, ALU.max))
                link(dve.tensor_tensor(hot, eq, over(scratch, n), ALU.is_equal))

            logit = rt[:, 0, :, :]
            gl, el = logit[:, :, 0:NG], logit[:, :, NG:NL]
            eq, masked, hot1, hot2, part = (rt[:, i, :, 0:NE] for i in range(1, 6))
            geq, ghot, pen = (rt[:, i, :, 0:NG] for i in range(6, 9))
            gtop, top1, top2, tmp, gsum, w1, w2 = (rs[:, i, :] for i in range(7))
            dve.wait_ge(logit_ps, 1)
            link(dve.tensor_tensor(logit, bank[4][:, 0:TT * NL].rearrange("p (t n) -> p t n", t=TT),
                                   rbias[:, :].unsqueeze(1).to_broadcast([P, TT, NL]), ALU.add))
            first_max(gl, group_key[:, :], NG, gtop, geq, ghot, tmp)
            link(dve.tensor_scalar(pen, ghot, -MASKED, MASKED, ALU.mult, ALU.add))
            link(dve.tensor_tensor(masked.rearrange("p t (g e) -> p t g e", g=NG),
                                   el.rearrange("p t (g e) -> p t g e", g=NG),
                                   pen.unsqueeze(3).to_broadcast([P, TT, NG, EPG]), ALU.add))
            first_max(masked, expert_key[:, :], NE, top1, eq, hot1, tmp)
            link(dve.scalar_tensor_tensor(masked, hot1, 100.0 * MASKED, masked, ALU.mult, ALU.add))
            first_max(masked, expert_key[:, :], NE, top2, eq, hot2, tmp)
            dve.tensor_tensor(chosen[:, :, :], hot1, hot2, ALU.add).then_inc(routed, 1)
            dve.tensor_tensor(e_in[:, :, 0:NG], gl, over(gtop, NG), ALU.subtract)
            dve.tensor_tensor(e_in[:, :, NG], top2, top1, ALU.subtract).then_inc(gexp_in, 1)
            dve.wait_ge(rank_ps, 1)
            ranks = bank[5][:, 0:TT * NE].rearrange("p (t n) -> p t n", t=TT)
            link(dve.scalar_tensor_tensor(rank[:, :, :], ranks, FAR, chosen[:, :, :], ALU.add, ALU.mult))
            counts = bank[5][0:1, TT * NE:(TT + 1) * NE].rearrange("p (q e) -> p q e", q=NQ)
            rf, ri = rounds_f[0:1, :, :], rounds_i[0:1, 0, 0:NQ]
            dve.tensor_reduce(rf[:, 0, NQ:2 * NQ], counts, AX.X, ALU.max).then_inc(rank_read, 1)
            link(dve.tensor_scalar(rank[:, :, :], rank[:, :, :], -FAR, None, ALU.add))

            def pick_slots(quad):
                for t in range(TT):
                    dve.tensor_tensor(pick[:, t, :, :],
                                      slot_id[:, :].unsqueeze(1).to_broadcast([P, QE, SLOTS]),
                                      rank[:, t, bass.ds(quad * QE, QE)].unsqueeze(2).to_broadcast(
                                          [P, QE, SLOTS]), ALU.is_equal).then_inc(pick_done, 1)

            pick_slots(0)
            link(dve.tensor_scalar(ri, rf[:, 0, NQ:2 * NQ], float(SLOTS - 1), None, ALU.add))
            link(dve.tensor_scalar(ri, ri, SLOTS.bit_length() - 1, None, ALU.logical_shift_right))
            link(dve.tensor_scalar(rf[:, 0, NQ:2 * NQ], ri, 1.0, None, ALU.max))
            for i in range(3):
                d = 1 << i
                link(dve.tensor_tensor(rf[:, i + 1, NQ:2 * NQ], rf[:, i, NQ:2 * NQ],
                                       rf[:, i, NQ - d:2 * NQ - d], ALU.add))
            n_c = MAX_ROUNDS + 1
            link(dve.tensor_tensor(passed[0:1, :, :], round_id[0:1, :].unsqueeze(2).to_broadcast([1, n_c, NQ]),
                                   rf[:, 3, NQ:2 * NQ].unsqueeze(1).to_broadcast([1, n_c, NQ]), ALU.is_ge))
            link(dve.tensor_reduce(quad_f[0:1, :], passed[0:1, :, :], AX.X, ALU.add))
            dve.tensor_scalar(quad_of[0:1, :], quad_f[0:1, :], float(NQ - 1), None, ALU.min)
            dve.tensor_scalar(bounds[0:1, NQ + 1:NQ + 2], rf[:, 3, 2 * NQ - 1:2 * NQ], -1.0, None, ALU.add)
            dve.tensor_copy(bounds[0:1, 0:NQ + 1], rf[:, 3, NQ - 1:2 * NQ]).then_inc(rounds_done, 1)

            def take_gathered(n):
                dve.wait_ge(xg_ps, 2 * n)
                dve.tensor_copy(xg[:, KC // 2:KC, :],
                                bank[5][:, :].rearrange("p (k s) -> p k s", s=P)).then_inc(xg_v, 1)

            take_gathered(1)
            dve.wait_ge(gexp_done, 1)
            link(dve.tensor_reduce(gsum, e_out[:, :, 0:NG], AX.X, ALU.add))
            link(dve.scalar_tensor_tensor(w1, e_out[:, :, NG], 1.0, gsum, ALU.add, ALU.mult))
            link(dve.reciprocal(w1, w1))
            link(dve.tensor_tensor(w2, w1, e_out[:, :, NG], ALU.mult))
            dve.tensor_tensor(comb[:, :, :], hot1, over(w1, NE), ALU.mult)
            link(dve.tensor_tensor(part, hot2, over(w2, NE), ALU.mult))
            link(dve.tensor_tensor(comb[:, :, :], comb[:, :, :], part, ALU.add))

            def weigh_slots(n, quad):
                dve.wait_ge(pick_done, 2 * n)
                for t in range(TT):
                    dve.tensor_tensor(pickw[:, t, :, :], pick[:, t, :, :],
                                      comb[:, t, bass.ds(quad * QE, QE)].unsqueeze(2).to_broadcast(
                                          [P, QE, SLOTS]), ALU.mult).then_inc(pickw_done, 1)
                dve.tensor_scalar(rank[:, :, bass.ds(quad * QE, QE)], rank[:, :, bass.ds(quad * QE, QE)],
                                  float(-SLOTS), None, ALU.add).then_inc(round_link, 1)

            def compute(c, coming):
                dve.wait_ge(round_link, 2 * c + 1)
                dve.wait_ge(pickw_done, 2 * c + 2)
                pick_slots(coming)
                dve.wait_ge(sg_done, c + 1)
                dve.tensor_tensor(hs[:, :], sg[:, :], bank[6][:, 0:DE],
                                  ALU.mult).then_inc(round_link, 1)
                dve.wait_ge(round_link, 2 * c + 2)
                dve.tensor_tensor(hs[:, :], hs[:, :], bank[6][:, DE:2 * DE],
                                  ALU.mult).then_inc(bank_free[6], 1)
                dve.wait_ge(y_ps, 2 * c + 2)
                dve.tensor_copy(ys[:, HALF:DM], bank[5][:, :]).then_inc(bank_free[5], 1)

            weigh_slots(1, 0)
            dve.wait_ge(rounds_done, 1)
            total = dve.value_load(bounds[0:1, NQ:NQ + 1], min_val=NQ, max_val=MAX_ROUNDS)
            last = dve.value_load(bounds[0:1, NQ + 1:NQ + 2], min_val=NQ - 1, max_val=MAX_ROUNDS)
            with dve.Fori(0, last) as c:
                coming = dve.value_load(quad_of[0:1, bass.ds(c + 1, 1)], min_val=0, max_val=NQ - 1)
                compute(c, coming)
                take_gathered(c + 2)
                weigh_slots(c + 2, coming)
            compute(last, NQ - 1)
            dve.wait_ge(added, 4 * total + 2)
            for t in range(TT):
                dve.bn_stats(stats[:, t, 0, :], bank[2 * t][:, :])
            for t in range(TT):
                dve.wait_ge(added, 4 * total + 3 + t)
                link(dve.bn_stats(stats[:, t, 1, :], bank[2 * t + 1][:, :]))
                variance(t)
            dve.wait_ge(ln_in, 64)
            for t in range(TT):
                halves = [(h, slice(h * HALF, (h + 1) * HALF)) for h in range(2 - t)]
                for h, cols in halves:
                    ins = dve.scalar_tensor_tensor(result[:, t, cols], bank[2 * t + h][:, :], moments[:, t, 0:1],
                                                   lng[:, cols], ALU.subtract, ALU.mult)
                link(ins)
                dve.wait_ge(rstd_done, TT + t + 1)
                for h, cols in halves:
                    dve.scalar_tensor_tensor(result[:, t, cols], result[:, t, cols], rstd[:, t:t + 1],
                                             lnb[:, cols], ALU.mult, ALU.add).then_inc(x1_done, 1)

        @block.tensor
        def _(pe):
            def low_words(n):
                s = n % NSPL
                return (wh[:, s, :].rearrange("p (k c) -> p k c", k=KC),
                        wl[:, s, :].rearrange("p (k c) -> p k c", k=KC))

            def product(dst, n, ks, high_in, low_in):
                h, l = low_words(n)
                for i, k in enumerate(ks):
                    if n == 0 and k % 2 == 0:
                        pe.wait_ge(xl_done, k // 2 + 1)
                    for w, v in ((h, high_in), (h, low_in), (l, high_in)):
                        mm = pe.matmul(dst, w[:, k, :], v[:, i, :], start=(i == 0 and w is h and v is high_in),
                                       stop=(i == len(ks) - 1 and w is l))
                return mm

            def seed(signal):
                for t in range(TT):
                    for h in range(2):
                        mm = pe.matmul(bank[2 * t + h][:, :], alpha_i[:, :], x1[:, t, h * HALF:(h + 1) * HALF],
                                       start=True, stop=True, skip_group_check=True)
                        if signal:
                            mm.then_inc(added, 1)

            def attention(i):
                c = i // 3
                if i % 3 == 0 and 1 <= c <= CC:
                    d = c - 1
                    if d >= 1:
                        pe.wait_ge(pT_done, 2 * d)
                    for j in range(2):
                        pe.wait_ge(prob_done, 2 * d + j + 1)
                        for b in range(3):
                            mm = pe.transpose(bank[2 + j][:, b * P:(b + 1) * P], sc[:, j, b, :], ident[:, :])
                        mm.then_inc(pT_ps, 1)
                if i % 3 == 0 and c < CC:
                    if c >= 1:
                        pe.wait_ge(score_sb, 2 * c)
                    for j in range(2):
                        hp = slice(HD * j, HD * (j + 1))
                        pe.matmul(bank[j][:, 0:P], qT[hp, c, 0:P], kT[hp, c, 0:P], start=True, stop=True)
                    for j in range(2):
                        hp = slice(HD * j, HD * (j + 1))
                        pe.matmul(bank[j][:, P:3 * P], qT[hp, c, P:SEQ], kT[hp, c, :],
                                  start=True, stop=True).then_inc(score_ps, 1)
                if i % 3 == 2 and 1 <= c <= CC:
                    d = c - 1
                    pe.wait_ge(pT_done, 2 * d + 2)
                    if d >= 2:
                        pe.wait_ge(ol_done, d - 1)
                    for b, keys in ((0, slice(0, 2)), (1, slice(2, 3))):
                        for j in range(2):
                            dst = bank[6 + d % 2][HD * j:HD * (j + 1), b * P:SEQ]
                            cols = slice((2 * d + j) * HD, (2 * d + j + 1) * HD)
                            mm = pe.matmul(dst, vv[:, b, cols],
                                           pT[:, j, keys, :].rearrange("p b q -> p (b q)"),
                                           start=(b == 0), stop=(b == 1), skip_group_check=True)
                    mm.then_inc(pv_ps, 1)

            def stay_warm(n, b=7):
                for _ in range(n):
                    pe.matmul(bank[b][:, 0:P], ident[:, :], ident[:, :], start=True, stop=True)

            pe.wait_ge(ident_done, 1)
            stay_warm(WARM_X)
            pe.wait_ge(x_in, 16 * TT)
            for b in range(KC // 2):
                for k in (2 * b, 2 * b + 1):
                    for t in range(TT):
                        mm = pe.transpose(bank[b][:, (k % 2) * SEQ + t * P:(k % 2) * SEQ + (t + 1) * P],
                                          x1[:, t, k::KC], ident[:, :])
                mm.then_inc(xT_ps, 1)
            stay_warm(WARM_UNIT)
            for n in range(U0):
                kind, c = unit(n)
                if n >= UA:
                    if n == UA:
                        pe.wait_ge(evac_a, UA)
                    attention(n - UA)
                if n == U0 - 1:
                    pe.wait_ge(consts, N_CONSTS)
                    pe.wait_ge(score_sb, NH)
                    pe.wait_ge(pT_done, NH)
                    seed(False)
                pe.wait_ge(lo_done, n + 1)
                if n < 2 * NA:
                    if n >= 2:
                        on_act, count = evacuated(n - 2)
                        pe.wait_ge(evac_a if on_act else evac_v, count)
                    dst = bank[4 + n % 2][:, 0:SEQ]
                else:
                    on_act, count = evacuated(2 * NA - 1 - (n == 2 * NA))
                    if c < 2 and kind == "ga":
                        pe.wait_ge(evac_a if on_act else evac_v, count)
                    half = 0 if kind == "ga" else 1
                    dst = bank[4 + n % 2][:, half * SEQ:(half + 1) * SEQ]
                if kind == "v":
                    t, s = n % 2, n // 2 * 2 % NSPL
                    if t == 0:
                        pe.wait_ge(lo_done, n + 2)
                    for k in range(KC):
                        ws = slice(k * P, (k + 1) * P)
                        for v, w in ((xh, wh), (xh, wl), (xl, wh)):
                            mm = pe.matmul(dst, v[:, k, t * P:(t + 1) * P], w[:, s:s + 2, ws],
                                           start=(k == 0 and v is xh and w is wh),
                                           stop=(k == KC - 1 and v is xl))
                else:
                    mm = product(dst, n, range(KC), xh, xl)
                mm.then_inc(unit_done, 1)

            def branches(j, m):
                pe.wait_ge(lo_done, UPJ * j + U0 + m + 1)
                product(bank[6 + m][:, 0:SEQ], U0 + m, range(CC), zh, zl)
                product(bank[6 + m][:, SEQ:2 * SEQ], U0 + m, range(CC, KC), oh, ol).then_inc(unit_done, 1)

            def merge(j, m, at, in_loop=True):
                n = U0 + at + m
                pe.wait_ge(lo_done, UPJ * j + n + 1)
                pe.wait_ge(yl_done, 2 * j + m + 1)
                s = n % NSPL
                for t in range(TT):
                    for v, w in ((yh, wh), (yh, wl), (yl, wh)):
                        for h in range(2):
                            mm = pe.matmul(bank[2 * t + h][:, :], v[:, m, t * P:(t + 1) * P],
                                           w[:, s, h * HALF:(h + 1) * HALF],
                                           start=False, stop=True, skip_group_check=True)
                    if m == 1 and not in_loop:
                        mm.then_inc(acc_done, 1)
                if in_loop or m == 0:
                    mm.then_inc(unit_done, 1)

            pe.wait_ge(ol_done, CC)
            pe.wait_ge(zl_done, CC)
            with pe.Fori(0, JP - 1) as j:
                for m in range(2):
                    branches(j, m)
                pe.wait_ge(sig_done, 2 * j + 2)
                for i in range(2, 6):
                    pe.wait_ge(lo_done, UPJ * j + U0 + i + 1)
                    half = i // 2 - 1
                    product(bank[4 + i % 2][:, half * SEQ:(half + 1) * SEQ], U0 + i, range(KC),
                            xh, xl).then_inc(unit_done, 1)
                for m in range(2):
                    merge(j, m, 6)
            for m in range(2):
                branches(JP - 1, m)
            for m in range(2):
                merge(JP - 1, m, 2, False)

            pe.wait_ge(y_done, KC)
            pe.wait_ge(wrb_done, 1)
            for k in range(KC):
                mm = pe.matmul(bank[6][:, 0:NL], ones[:, :], wrb[:, k, :],
                               start=(k == 0), stop=(k == KC - 1))
            mm.then_inc(bias_ps, 1)

            def transpose_tile(t):
                pe.wait_ge(norm_done[t], 2)
                for k in range(KC):
                    mm = pe.transpose(bank[4 + 2 * t + k // 4][:, (k % 4) * P:(k % 4 + 1) * P],
                                      x1[:, t, k::KC], ident[:, :])
                    if k % 4 == 3:
                        mm.then_inc(x1T_ps, 1)

            def logits(t, g):
                pe.wait_ge(bank_free[4 + 2 * t + g], 1)
                for k in range(g * KC // 2, (g + 1) * KC // 2):
                    mm = pe.matmul(bank[4][:, t * NL:(t + 1) * NL], x1T[:, k, t * P:(t + 1) * P],
                                   wr[:, k, :], start=(k == 0), stop=(k == KC - 1), skip_group_check=True)
                return mm

            stay_warm(WARM_NORM)
            transpose_tile(0)
            pe.wait_ge(bias_read, 1)
            logits(0, 0)
            transpose_tile(1)
            logits(0, 1)
            logits(1, 0)
            logits(1, 1).then_inc(logit_ps, 1)
            pe.wait_ge(x1_done, X1_PARTS)
            seed(True)
            pe.wait_ge(routed, 1)
            first, second = chosen[:, 0, :], chosen[:, 1, :]
            pe.matmul(bank[5][:, 0:NE], before[:, :], first, start=True, stop=True)
            pe.matmul(bank[5][:, NE:2 * NE], ones_b[:, :], first, start=True, stop=False)
            pe.matmul(bank[5][:, NE:2 * NE], before[:, :], second, start=False, stop=True)
            pe.matmul(bank[5][:, TT * NE:(TT + 1) * NE], ones_b[:, :], first, start=True, stop=False)
            pe.matmul(bank[5][:, TT * NE:(TT + 1) * NE], ones_b[:, :], second,
                      start=False, stop=True).then_inc(rank_ps, 1)

            def gather(c):
                pe.wait_ge(pick_done, 2 * c + 2)
                for k in range(KC):
                    for t in range(TT):
                        mm = pe.matmul(bank[4 + k // 4][:, (k % 4) * P:(k % 4 + 1) * P], x1[:, t, k::KC],
                                       pick[:, t, :, :].rearrange("p e s -> p (e s)"),
                                       start=(t == 0), stop=(t == TT - 1))
                    if k % 4 == 3:
                        mm.then_inc(xg_ps, 1)

            pe.wait_ge(rank_read, 1)
            gather(0)
            pe.wait_ge(rounds_done, 1)
            with pe.Fori(0, NQ // 2) as o:
                for half in range(2):
                    q = 2 * o + half
                    w = gu[half]
                    first = pe.value_load(bounds[0:1, bass.ds(q, 1)], min_val=0, max_val=MAX_ROUNDS)
                    end = pe.value_load(bounds[0:1, bass.ds(q + 1, 1)], min_val=1, max_val=MAX_ROUNDS)
                    with pe.Fori(first, end) as c:
                        pe.wait_ge(xg_a, c + 1)
                        pe.wait_ge(xg_v, c + 1)
                        pe.wait_ge(bank_free[6], c + 1)
                        for k in range(KC):
                            if k in (0, K_FIRST):
                                pe.wait_ge(gu_in[half][k // K_FIRST], 2 * QE * 16 * (o + 1))
                            for e in range(QE):
                                g = slice(SLOTS * e, SLOTS * (e + 1))
                                mm = pe.matmul(bank[6][g, :], xg[:, k, g], w[:, e, k, :],
                                               start=(k == 0), stop=(k == KC - 1))
                            if k == K_FIRST - 1:
                                mm.then_inc(gu_part, 1)
                        mm.then_inc(gu_ps, 1)
                        pe.wait_ge(bank_free[7], c + 1)
                        pe.wait_ge(pickw_done, 2 * c + 2)
                        for t in range(TT):
                            mm = pe.transpose(bank[7][:, SEQ + t * P:SEQ + (t + 1) * P],
                                              pickw[:, t, :, :].rearrange("p e s -> p (e s)"), ident[:, :])
                        mm.then_inc(put_ps, 1)
                        stay_warm(WARM_ROUND[0], 5)
                        pe.wait_ge(bank_free[6], c + 2)
                        pe.wait_ge(put_done, c + 1)
                        for j in range(FC):
                            mm = pe.transpose(bank[7][:, j * P:(j + 1) * P], hs[:, j * P:(j + 1) * P],
                                              ident[:, :])
                        mm.then_inc(hT_ps, 1)
                        stay_warm(WARM_ROUND[1], 5)
                        pe.wait_ge(bank_free[7], c + 2)
                        for h in range(2):
                            pe.wait_ge(dn_in[h], QE * 16 * (q + 1))
                            for j in range(FC):
                                for e in range(QE):
                                    g = slice(SLOTS * e, SLOTS * (e + 1))
                                    mm = pe.matmul(bank[4 + h][g, :], hT[:, j, g],
                                                   dn[:, e, j, h * HALF:(h + 1) * HALF],
                                                   start=(j == 0), stop=(j == FC - 1))
                            mm.then_inc(y_ps, 1)
                        for h in range(2):
                            pe.wait_ge(bank_free[4 + h], c + 2)
                            for t in range(TT):
                                pe.matmul(bank[2 * t + h][:, :], put[:, t * P:(t + 1) * P],
                                          ys[:, h * HALF:(h + 1) * HALF], start=False, stop=True,
                                          skip_group_check=True).then_inc(added, 1)
                        gather(c + 1)


_INS = ['x', 'w_in', 'conv_w', 'w_out_conv', 'w_out_attn', 'w_o', 'ln1_g', 'ln1_b',
        'w_router_group', 'w_router_expert', 'w_gate', 'w_up', 'w_down', 'ln2_g', 'ln2_b']


def kernel(**inputs):
    import numpy as _np
    import concourse.bacc as _bacc
    from concourse import mybir as _mybir
    from concourse.bass_utils import run_bass_kernel_spmd as _run

    nc = _bacc.Bacc("TRN2", target_bir_lowering=False, num_devices=1)
    arrays, args = {}, []
    for name in _INS:
        a = _np.ascontiguousarray(inputs[name])
        arrays[f"in_{name}"] = a
        args.append(nc.dram_tensor(f"in_{name}", a.shape, _mybir.dt.from_np(a.dtype),
                                   kind="ExternalInput").ap())
    args.append(nc.dram_tensor("out_0", (1, SEQ, DM), _mybir.dt.float32, kind="ExternalOutput").ap())
    hybrid_block(nc, *args)
    r = _run(nc, [arrays], core_ids=[0])
    return r.results[0]["out_0"]
```
